# Optimizing a Trainium2 kernel written in Bass

```python
import jax, jax.numpy as jnp
from jax import lax
import numpy as np

D_MODEL = 1024
BATCH = 1
SEQ = 256
DEPTH = 2

N_A_LAYERS = DEPTH // 2
N_B_LAYERS = DEPTH - N_A_LAYERS
N_DENSE = (DEPTH + 1) // 2
N_MOE = DEPTH // 2
RMS_EPS = 1e-6
A_HEADS = 4
A_INNER = D_MODEL
A_HEAD_DIM = A_INNER // A_HEADS
A_CONV = 4
A_CHUNK = 64
B_HEADS = 16
B_HEAD_DIM = D_MODEL // B_HEADS
B_KV_GROUPS = 4
B_REP = B_HEADS // B_KV_GROUPS
CMP_LEN = 32
CMP_STRIDE = 16
CMP_HIDDEN = 256
SEL_BLOCK = 64
SEL_TOPN = 16
WINDOW = 512
NSA_Q_BLOCK = 32
FORCED_SCORE = 1e4
FFN_DENSE = 2816
N_EXPERTS = 8
TOP_K = 2
FFN_EXPERT = 3584
FFN_TOKEN_BLOCK = 128

kernel_name = "yoco_mlstm_nsa_moe_block"

def rmsnorm(x, g):
    xf = x.astype(jnp.float32)
    y = xf * lax.rsqrt(jnp.mean(xf * xf, axis=-1, keepdims=True) + RMS_EPS) * g.astype(jnp.float32)
    return y.astype(x.dtype)

def alibi_slopes(n):
    return jnp.asarray(np.power(2.0, -8.0 * np.arange(1, n + 1) / n).astype(np.float32))

def safe_softmax(s):
    m = jnp.max(s, axis=-1, keepdims=True)
    m = jnp.where(jnp.isfinite(m), m, 0.0)
    e = jnp.exp(s - m)
    d = jnp.sum(e, axis=-1, keepdims=True)
    return e / jnp.where(d > 0, d, 1.0)

def causal_dwconv(x, w):
    K = w.shape[0]
    T = x.shape[1]
    xp = jnp.pad(x, ((0, 0), (K - 1, 0), (0, 0)))
    y = xp[:, 0:T] * w[0]
    for j in range(1, K):
        y = y + xp[:, j:j + T] * w[j]
    return y

def _mlstm_chunk(carry, inp):
    c, n, m = carry
    q, k, v, log_i, log_f = inp
    L = q.shape[2]
    causal = jnp.tril(jnp.ones((L, L), dtype=bool))
    b = jnp.cumsum(log_f, axis=-1)
    d = jnp.where(causal, b[..., :, None] - b[..., None, :] + log_i[..., None, :], -jnp.inf)
    inter = b + m[..., None]
    m_t = jnp.maximum(inter, jnp.max(d, axis=-1))
    w_intra = jnp.exp(d - m_t[..., None])
    w_inter = jnp.exp(inter - m_t)
    s = jnp.einsum('bhtd,bhsd->bhts', q, k) * w_intra
    num = jnp.einsum('bhts,bhsd->bhtd', s, v) + w_inter[..., None] * jnp.einsum('bhvk,bhtk->bhtv', c, q)
    den = jnp.sum(s, axis=-1) + w_inter * jnp.einsum('bhk,bhtk->bht', n, q)
    h = num / jnp.maximum(jnp.abs(den), jnp.exp(-m_t))[..., None]
    b_last = b[..., -1]
    g = b_last[..., None] - b + log_i
    m_new = jnp.maximum(b_last + m, jnp.max(g, axis=-1))
    a_prev = jnp.exp(b_last + m - m_new)
    a_s = jnp.exp(g - m_new[..., None])
    c_new = a_prev[..., None, None] * c + jnp.einsum('bhsv,bhsk->bhvk', v * a_s[..., None], k)
    n_new = a_prev[..., None] * n + jnp.einsum('bhs,bhsk->bhk', a_s, k)
    return (c_new, n_new, m_new), h

def mlstm_mixer(h, w_in, b_gate, conv_w, g_out, w_out):
    B, T, _ = h.shape
    f32 = jnp.float32
    proj = h @ w_in
    qk = causal_dwconv(proj[..., :2 * A_INNER], conv_w)
    q = qk[..., :A_INNER]
    k = qk[..., A_INNER:]
    v = proj[..., 2 * A_INNER:3 * A_INNER]
    o = proj[..., 3 * A_INNER:4 * A_INNER]
    gl = (proj[..., 4 * A_INNER:] + b_gate).astype(f32)
    log_i = gl[..., :A_HEADS]
    log_f = jax.nn.log_sigmoid(gl[..., A_HEADS:])
    nc = T // A_CHUNK

    def to_chunks(a):
        return a.astype(f32).reshape(B, nc, A_CHUNK, A_HEADS, A_HEAD_DIM).transpose(1, 0, 3, 2, 4)

    def gate_chunks(a):
        return a.reshape(B, nc, A_CHUNK, A_HEADS).transpose(1, 0, 3, 2)

    qc = to_chunks(q)
    kc = to_chunks(k) * (A_HEAD_DIM ** -0.5)
    vc = to_chunks(v)
    init = (jnp.zeros((B, A_HEADS, A_HEAD_DIM, A_HEAD_DIM), f32),
            jnp.zeros((B, A_HEADS, A_HEAD_DIM), f32),
            jnp.zeros((B, A_HEADS), f32))
    _, hc = lax.scan(_mlstm_chunk, init, (qc, kc, vc, gate_chunks(log_i), gate_chunks(log_f)))
    hs = hc.transpose(1, 0, 3, 2, 4).reshape(B, T, A_HEADS, A_HEAD_DIM)
    hs = hs * lax.rsqrt(jnp.mean(hs * hs, axis=-1, keepdims=True) + RMS_EPS)
    hs = hs.reshape(B, T, A_INNER) * g_out.astype(f32) * jax.nn.sigmoid(o.astype(f32))
    return hs.astype(h.dtype) @ w_out

def nsa_shared_kv(hkv, w_kv, cmp_pos, cmp_w1, cmp_w2):
    B, T, _ = hkv.shape
    G, Dh = B_KV_GROUPS, B_HEAD_DIM
    kv = (hkv @ w_kv).reshape(B, T, 6, G, Dh)
    n_cmp = (T - CMP_LEN) // CMP_STRIDE + 1
    idx = np.arange(n_cmp)[:, None] * CMP_STRIDE + np.arange(CMP_LEN)[None, :]
    blk = kv[:, idx, :2]
    blk = blk + cmp_pos[None, None, :, :, None, :]
    blk = blk.transpose(0, 3, 4, 1, 2, 5).reshape(B, 2, G, n_cmp, CMP_LEN * Dh)
    hid = jax.nn.silu(jnp.einsum('bcgnf,cfh->bcgnh', blk, cmp_w1))
    kvc = jnp.einsum('bcgnh,chd->bcgnd', hid, cmp_w2)
    n_sel = T // SEL_BLOCK
    k_slc = kv[:, :, 2].transpose(0, 2, 1, 3).reshape(B, G, n_sel, SEL_BLOCK, Dh)
    v_slc = kv[:, :, 3].transpose(0, 2, 1, 3).reshape(B, G, n_sel, SEL_BLOCK, Dh)
    pad = ((0, 0), (0, 0), (WINDOW, 0), (0, 0))
    k_win = jnp.pad(kv[:, :, 4].transpose(0, 2, 1, 3), pad)
    v_win = jnp.pad(kv[:, :, 5].transpose(0, 2, 1, 3), pad)
    return (kvc[:, 0], kvc[:, 1], k_slc, v_slc, k_win, v_win)

def nsa_mixer(h, shared, w_q, b_gate, w_out):
    k_cmp, v_cmp, k_slc, v_slc, k_win, v_win = shared
    B, T, _ = h.shape
    G, R, Dh = B_KV_GROUPS, B_REP, B_HEAD_DIM
    HD = B_HEADS * Dh
    f32 = jnp.float32
    scale = Dh ** -0.5
    proj = h @ w_q
    q = proj[..., :HD].reshape(B, T, G, R, Dh).transpose(0, 2, 3, 1, 4)
    gates = jax.nn.sigmoid((proj[..., HD:] + b_gate).astype(f32))
    gates = gates.reshape(B, T, G, R, 3).transpose(0, 2, 3, 1, 4)
    slopes = alibi_slopes(B_HEADS).reshape(G, R)
    sl5 = slopes[None, :, :, None, None]
    sl6 = slopes[None, :, :, None, None, None]
    n_cmp = k_cmp.shape[2]
    n_sel = k_slc.shape[2]
    n_top = min(SEL_TOPN, n_sel)
    cmp_end = jnp.arange(n_cmp) * CMP_STRIDE + (CMP_LEN - 1)
    ci = np.arange(n_cmp)[:, None] * CMP_STRIDE
    sj = np.arange(n_sel)[None, :] * SEL_BLOCK
    overlap = jnp.asarray(((ci < sj + SEL_BLOCK) & (ci + CMP_LEN > sj)).astype(np.float32))
    blk_j = jnp.arange(n_sel)
    bi = jnp.arange(B)[:, None, None, None]
    gi = jnp.arange(G)[None, :, None, None]
    QB = NSA_Q_BLOCK

    def block_fn(iq):
        t0 = iq * QB
        tpos = t0 + jnp.arange(QB)
        qb = lax.dynamic_slice_in_dim(q, t0, QB, axis=3)
        gb = lax.dynamic_slice_in_dim(gates, t0, QB, axis=3)
        dist_c = (tpos[:, None] - cmp_end[None, :]).astype(f32)
        s_c = jnp.einsum('bgrqd,bgcd->bgrqc', qb, k_cmp).astype(f32) * scale - sl5 * dist_c
        p_cmp = safe_softmax(jnp.where(dist_c >= 0, s_c, -jnp.inf))
        o_cmp = jnp.einsum('bgrqc,bgcd->bgrqd', p_cmp, v_cmp)
        imp = jnp.einsum('bgrqc,cj->bgqj', p_cmp, overlap)
        cur = tpos // SEL_BLOCK
        forced = (blk_j[None, :] == 0) | (blk_j[None, :] == cur[:, None]) | (blk_j[None, :] == cur[:, None] - 1)
        valid = blk_j[None, :] * SEL_BLOCK <= tpos[:, None]
        imp = jnp.where(forced[None, None], FORCED_SCORE, imp)
        imp = jnp.where(valid[None, None], imp, -jnp.inf)
        _, idx = lax.top_k(imp, n_top)
        ks = k_slc[bi, gi, idx]
        vs = v_slc[bi, gi, idx]
        kpos = idx[..., None] * SEL_BLOCK + jnp.arange(SEL_BLOCK)
        dist_s = (tpos[:, None, None] - kpos).astype(f32)
        s_s = jnp.einsum('bgrqd,bgqnkd->bgrqnk', qb, ks).astype(f32) * scale - sl6 * dist_s[:, :, None]
        s_s = jnp.where((dist_s >= 0)[:, :, None], s_s, -jnp.inf).reshape(B, G, R, QB, n_top * SEL_BLOCK)
        p_s = safe_softmax(s_s)
        o_slc = jnp.einsum('bgrqk,bgqkd->bgrqd', p_s, vs.reshape(B, G, QB, n_top * SEL_BLOCK, Dh))
        kw = lax.dynamic_slice_in_dim(k_win, t0, WINDOW + QB, axis=2)
        vw = lax.dynamic_slice_in_dim(v_win, t0, WINDOW + QB, axis=2)
        spos = t0 - WINDOW + jnp.arange(WINDOW + QB)
        dist_w = tpos[:, None] - spos[None, :]
        mask_w = (dist_w >= 0) & (dist_w < WINDOW) & (spos[None, :] >= 0)
        s_w = jnp.einsum('bgrqd,bgkd->bgrqk', qb, kw).astype(f32) * scale - sl5 * dist_w.astype(f32)
        p_w = safe_softmax(jnp.where(mask_w, s_w, -jnp.inf))
        o_win = jnp.einsum('bgrqk,bgkd->bgrqd', p_w, vw)
        return gb[..., 0:1] * o_cmp + gb[..., 1:2] * o_slc + gb[..., 2:3] * o_win

    outs = lax.map(block_fn, jnp.arange(T // QB))
    o = outs.transpose(1, 0, 4, 2, 3, 5).reshape(B, T, HD)
    return o.astype(h.dtype) @ w_out

def token_block_map(fn, x):
    B, T, D = x.shape
    nb = T // FFN_TOKEN_BLOCK
    xb = x.reshape(B, nb, FFN_TOKEN_BLOCK, D).transpose(1, 0, 2, 3).reshape(nb, B * FFN_TOKEN_BLOCK, D)
    yb = lax.map(fn, xb)
    return yb.reshape(nb, B, FFN_TOKEN_BLOCK, D).transpose(1, 0, 2, 3).reshape(B, T, D)

def swiglu_dense(h, w_gu, w_down):
    def fn(t):
        gu = t @ w_gu
        return (jax.nn.silu(gu[..., :FFN_DENSE]) * gu[..., FFN_DENSE:]) @ w_down
    return token_block_map(fn, h)

def moe_swiglu(h, w_router, w_gu, w_down):
    def fn(t):
        logits = (t @ w_router).astype(jnp.float32)
        top_v, top_i = lax.top_k(logits, TOP_K)
        top_w = jax.nn.softmax(top_v, axis=-1)
        gate = jnp.sum(jax.nn.one_hot(top_i, N_EXPERTS, dtype=jnp.float32) * top_w[..., None], axis=1)
        gu = jnp.einsum('nd,edf->nef', t, w_gu)
        act = jax.nn.silu(gu[..., :FFN_EXPERT]) * gu[..., FFN_EXPERT:] * gate[..., None].astype(t.dtype)
        return jnp.einsum('nef,efd->nd', act, w_down)
    return token_block_map(fn, h)

def setup_inputs(seed: int = 0) -> dict:
    key = jax.random.key(seed)
    ks = jax.random.split(key, 24)
    f32 = jnp.float32

    def nrm(k, shape, s):
        return jax.random.normal(k, shape, f32) * s

    D = D_MODEL
    HD = B_HEADS * B_HEAD_DIM
    GD = B_KV_GROUPS * B_HEAD_DIM
    i_bias = nrm(ks[4], (N_A_LAYERS, A_HEADS), 0.1)
    f_bias = jnp.linspace(3.0, 6.0, A_HEADS, dtype=f32)[None, :] + nrm(ks[5], (N_A_LAYERS, A_HEADS), 0.1)
    return {
        "x": nrm(ks[0], (BATCH, SEQ, D), 1.0),
        "norm_mix": 1.0 + nrm(ks[1], (DEPTH, D), 0.02),
        "norm_ffn": 1.0 + nrm(ks[2], (DEPTH, D), 0.02),
        "a_w_in": nrm(ks[3], (N_A_LAYERS, D, 4 * A_INNER + 2 * A_HEADS), D ** -0.5),
        "a_b_gate": jnp.concatenate([i_bias, f_bias], axis=-1),
        "a_conv": nrm(ks[6], (N_A_LAYERS, A_CONV, 2 * A_INNER), A_CONV ** -0.5),
        "a_norm_h": 1.0 + nrm(ks[7], (N_A_LAYERS, A_INNER), 0.02),
        "a_w_out": nrm(ks[8], (N_A_LAYERS, A_INNER, D), A_INNER ** -0.5),
        "norm_kv": 1.0 + nrm(ks[9], (D,), 0.02),
        "b_w_kv": nrm(ks[10], (D, 6 * GD), D ** -0.5),
        "b_cmp_pos": nrm(ks[11], (CMP_LEN, 2, B_HEAD_DIM), 0.02),
        "b_cmp_w1": nrm(ks[12], (2, CMP_LEN * B_HEAD_DIM, CMP_HIDDEN), (CMP_LEN * B_HEAD_DIM) ** -0.5),
        "b_cmp_w2": nrm(ks[13], (2, CMP_HIDDEN, B_HEAD_DIM), CMP_HIDDEN ** -0.5),
        "b_w_q": nrm(ks[14], (N_B_LAYERS, D, HD + 3 * B_HEADS), D ** -0.5),
        "b_b_gate": nrm(ks[15], (N_B_LAYERS, 3 * B_HEADS), 0.02),
        "b_w_out": nrm(ks[16], (N_B_LAYERS, HD, D), HD ** -0.5),
        "f_w_gu": nrm(ks[17], (N_DENSE, D, 2 * FFN_DENSE), D ** -0.5),
        "f_w_down": nrm(ks[18], (N_DENSE, FFN_DENSE, D), FFN_DENSE ** -0.5),
        "m_router": nrm(ks[19], (N_MOE, D, N_EXPERTS), D ** -0.5),
        "m_w_gu": nrm(ks[20], (N_MOE, N_EXPERTS, D, 2 * FFN_EXPERT), D ** -0.5),
        "m_w_down": nrm(ks[21], (N_MOE, N_EXPERTS, FFN_EXPERT, D), FFN_EXPERT ** -0.5),
        "norm_final": 1.0 + nrm(ks[22], (D,), 0.02),
    }

def reference(x, norm_mix, norm_ffn, a_w_in, a_b_gate, a_conv, a_norm_h, a_w_out, norm_kv, b_w_kv,
              b_cmp_pos, b_cmp_w1, b_cmp_w2, b_w_q, b_b_gate, b_w_out, f_w_gu, f_w_down,
              m_router, m_w_gu, m_w_down, norm_final):
    shared = None
    for i in range(DEPTH):
        if i < N_A_LAYERS:
            x = x + mlstm_mixer(rmsnorm(x, norm_mix[i]), a_w_in[i], a_b_gate[i], a_conv[i],
                                a_norm_h[i], a_w_out[i])
        else:
            if i == N_A_LAYERS:
                shared = nsa_shared_kv(rmsnorm(x, norm_kv), b_w_kv, b_cmp_pos, b_cmp_w1, b_cmp_w2)
            j = i - N_A_LAYERS
            x = x + nsa_mixer(rmsnorm(x, norm_mix[i]), shared, b_w_q[j], b_b_gate[j], b_w_out[j])
        hf = rmsnorm(x, norm_ffn[i])
        if i % 2 == 0:
            x = x + swiglu_dense(hf, f_w_gu[i // 2], f_w_down[i // 2])
        else:
            x = x + moe_swiglu(hf, m_router[i // 2], m_w_gu[i // 2], m_w_down[i // 2])
    return rmsnorm(x, norm_final)


_drawn_inputs = setup_inputs


def setup_inputs(seed=0):
    import zlib

    import numpy as np

    out = dict(_drawn_inputs(seed))
    spreads = {}
    factors = {'norm_kv': 2.724, 'b_cmp_pos': 3.321, 'b_b_gate': 5.025, 'norm_final': 2.824}
    for name, (base, spread) in spreads.items():
        noise = np.random.default_rng([zlib.crc32(name.encode()), seed]).standard_normal(out[name].shape)
        drawn = base * np.exp(spread * noise) if base else spread * noise
        out[name] = __import__('jax').numpy.asarray(drawn.astype(out[name].dtype))
    for name, factor in factors.items():
        out[name] = (out[name] * factor).astype(out[name].dtype)
    return out
```

```python
import concourse.bass as bass
from concourse import mybir
from contextlib import ExitStack

P = 128
D, T = 1024, 256
NT, KD = T // P, D // P
HA, DA = 4, 256
HB, DB, G, R = 16, 64, 4, 4
NC_, CL, CS = 15, 32, 16
CH = 256
FD, NE, FE = 2816, 8, 3584
EPS = 1e-6
NEG = -1e30
SLOT = 2048
RAW, SPLIT = 6, 3
NJ_MAX = 11
JOB_SLOTS = 7 * 4 + 14
XW = 2 * 16 * G * NC_ + 12
XM = G * NC_ + 12
AHEAD = 2

C_GAIN = 0
C_CONV = C_GAIN + 56
C_BIF = C_CONV + 64
C_BG = C_BIF + 2
C_POS = C_BG + 48
C_W2 = C_POS + 32
C_WS = C_W2 + 256
C_END = C_WS + 512


def trunk(nc, x, packed, a_w_in, a_w_out, b_w_kv, b_cmp_w1, b_w_q, b_w_out, f_w_gu, f_w_down,
          m_w_gu, m_w_down, norm_ffn1, norm_final, out, dbg=None):
    F32, FR, I32 = mybir.dt.float32, mybir.dt.float32r, mybir.dt.int32
    ALU, ACT, AX = mybir.AluOpType, mybir.ActivationFunctionType, mybir.AxisListType
    ctx = ExitStack()
    ctx.enter_context(nc.allow_non_contiguous_dma("weights"))

    edge = [(nc.sbuf_base + 31) // 32 * 32]

    def sb(name, shape, dt=F32, at=None):
        size = 4
        for n in shape[1:]:
            size *= n
        if at is None:
            at = edge[0]
            edge[0] = (at + size + 31) // 32 * 32
        return nc.alloc_sbuf_tensor_at(name, list(shape), dt, offset=at), at

    raw, _ = sb("raw", [P, RAW, SLOT])
    w_hi, _ = sb("w_hi", [P, SPLIT, SLOT], FR)
    w_lo, _ = sb("w_lo", [P, SPLIT, SLOT], FR)
    xs, _ = sb("xs", [P, NT, D])
    xn, _ = sb("xn", [P, NT, D])
    ht_hi, _ = sb("ht_hi", [P, KD, T], FR)
    ht_lo, _ = sb("ht_lo", [P, KD, T], FR)
    at_hi, a0 = sb("at_hi", [P, 22 * T], FR)
    at_lo, _ = sb("at_lo", [P, 22 * T], FR)
    arena_end = edge[0]
    sg, sg_at = sb("sg", [P, NT, 512])
    av, _ = sb("av", [P, NT, 512])
    pk, _ = sb("pk", [P, C_END])
    ws_hi, _ = sb("ws_hi", [P, KD, 64], FR)
    ws_lo, _ = sb("ws_lo", [P, KD, 64], FR)
    ident, _ = sb("ident", [P, P])
    tri_mask, _ = sb("tri_mask", [P, T])
    small, small_at = sb("small", [P, 512])
    sel_oh, _ = sb("sel_oh", [P, NT, P], FR)
    slot_iota, _ = sb("slot_iota", [P, P])
    rows, _ = sb("rows", [4, 8, T], F32, sg_at)

    o = a0
    qk, _ = sb("qk", [P, 16, T], F32, o); o += 16 * T * 4
    va, _ = sb("va", [P, NT, HA, DA + 1], F32, o); o += NT * HA * (DA + 1) * 4
    og, _ = sb("og", [P, NT, D], F32, o); o += NT * D * 4
    wd, _ = sb("wd", [P, HA, 384], F32, o); o += HA * 384 * 4
    pd, _ = sb("pd", [P, 2, 384], F32, o); o += 2 * 384 * 4
    assert o <= arena_end
    o = a0
    kt, _ = sb("kt", [P, 2, G, T], F32, o); o += 2 * G * T * 4
    vv, _ = sb("vv", [P, NT, 2, G * DB], F32, o); o += NT * 2 * G * DB * 4
    qt, _ = sb("qt", [P, 8, T], F32, o); o += 8 * T * 4
    ct_at = o
    ct, _ = sb("ct", [P, 2, G, T], F32, o); o += 2 * G * T * 4
    xf_at = o
    xf, _ = sb("xf", [P, XW], F32, o); o += (XW * 4 + 31) // 32 * 32
    vbd, _ = sb("vbd", [P, G, R * DB], F32, o); o += G * R * DB * 4
    hidt, _ = sb("hidt", [P, 2, 2, G * NC_], F32, o); o += 4 * G * NC_ * 4
    kc, _ = sb("kc", [P, G * NC_], F32, o); o += 64 * 4
    dat, _ = sb("dat", [P, NT, T], F32, o); o += NT * T * 4
    att, _ = sb("att", [P, 2, 2, 32], F32, o); o += 128 * 4
    gat, _ = sb("gat", [P, NT, 48], F32, o); o += 96 * 4
    coef, _ = sb("coef", [P, 2, 32], F32, o); o += 64 * 4
    assert o <= arena_end, (o, arena_end)
    xc_hi, _ = sb("xc_hi", [P, XW], FR, ct_at)
    xc_lo, _ = sb("xc_lo", [P, XW], FR, sg_at)
    hid, _ = sb("hid", [G * NC_, 2, CH], F32, small_at)
    sc, _ = sb("sc", [P, 3, 512], F32, xf_at)
    ptg = [sb("pt_even", [P, 4, R, P], F32, sg_at)[0], sb("pt_odd", [P, 4, R, P], F32, ct_at)[0]]
    pc, _ = sb("pc", [P, HB, 32], F32, small_at)
    hg_hi, _ = sb("hg_hi", [P, NT, D], FR, a0 + 28 * P * 4)
    hg_lo, _ = sb("hg_lo", [P, NT, D], FR, a0 + 22 * T * 4 + 28 * P * 4)
    gfb, _ = sb("gfb", [P, D])
    g1b, g1b_at = sb("g1b", [P, D])
    nsel, _ = sb("nsel", [4, HA, P], F32, g1b_at)
    pct, _ = sb("pct", [P, 512], F32, g1b_at)
    ysb, _ = sb("ysb", [P, D], F32, g1b_at)
    dcb, dcb_at = sb("dcb", [P, NT, HB, NC_])
    cval, _ = sb("cval", [P, NT, NC_])
    ones, _ = sb("ones", [P, P])
    tri1, _ = sb("tri1", [P, P])
    tri8, _ = sb("tri8", [P, NE, NE])
    selt, _ = sb("selt", [P, 2 * P + 1])
    iot, _ = sb("iot", [P, NE])
    tab, _ = sb("tab", [1, 16], I32)
    posj, _ = sb("posj", [P, NT, 12])
    gatej, _ = sb("gatej", [P, NT, 12])
    consts, _ = sb("consts", [P, 4])
    stats, _ = sb("stats", [P, 64])
    cmx, _ = sb("cmx", [P, 2, HB])
    big8, _ = sb("big8", [P, 2, NT * NE * NE], F32, dcb_at)
    rt, _ = sb("rt", [P, 16, NT * NE])
    assert edge[0] <= nc.sbuf_usable_end, edge[0]

    B = [ctx.enter_context(nc.psum_tensor(f"bank{i}", [P, 512], F32)) for i in range(8)]

    def sem(name):
        return ctx.enter_context(nc.semaphore(name))

    landed = [sem(f"landed{i}") for i in range(RAW)]
    s_hi, s_lo, s_used = sem("hi_ready"), sem("lo_ready"), sem("slot_used")
    s_x, s_pk, s_g1b, s_gfb = sem("x_landed"), sem("packed_landed"), sem("ffn_gain_landed"), sem("final_gain_landed")
    s_out = sem("out_stored")
    s_pc = sem("pool_chain"); s_ac = sem("act_chain"); s_dc = sem("dve_chain")
    s_const = sem("constants_ready")
    s_wshi, s_wslo = sem("small_hi"), sem("small_lo")
    s_sq, s_rstd, s_xn = sem("squares_summed"), sem("rstd_ready"), sem("xn_ready")
    s_xt, s_hth, s_htl = sem("transposed"), sem("ht_hi_ready"), sem("ht_lo_ready")
    s_y, s_xu = sem("y_ready"), sem("x_updated")
    s_gp, s_gsb, s_grow, s_rows = sem("gate_product"), sem("gate_copied"), sem("gate_rows"), sem("rows_ready")
    s_lnx, s_lnd = sem("softplus_in"), sem("softplus_out")
    s_cols, s_colc, s_nm, s_arg, s_wd = sem("gate_columns"), sem("columns_copied"), sem("max_rows"), sem("arg_ready"), sem("decay_ready")
    s_qka, s_conv = sem("tap_applied"), sem("conv_done")
    s_v, s_vc, s_o, s_oc = sem("v_product"), sem("v_copied"), sem("o_product"), sem("o_gated")
    s_s, s_p, s_num, s_den, s_hs = sem("scores"), sem("weighted"), sem("numerator"), sem("inv_den"), sem("h_scaled")
    s_hq, s_hr = sem("h_squares"), sem("h_rstd")
    s_g, s_silu, s_u, s_mul = sem("gate_half"), sem("silu_done"), sem("up_half"), sem("act_done")
    s_tp, s_tph, s_tpl = sem("act_transposed"), sem("at_hi_ready"), sem("at_lo_ready")
    s_kva, s_kvd = sem("kv_copied_act"), sem("kv_copied_dve")
    s_xf, s_xch, s_xcl = sem("blocks_ready"), sem("blocks_hi"), sem("blocks_lo")
    s_hid, s_hidt, s_hidc, s_w2, s_kc = sem("hidden_ready"), sem("hidden_transposed"), sem("hidden_t_copied"), sem("compressed"), sem("compressed_copied")
    s_qc = sem("q_copied")
    s_ng, s_ngb, s_nge, s_gat = sem("nsa_gates"), sem("nsa_gates_biased"), sem("nsa_gates_exp"), sem("gates_ready")
    s_cs, s_cb, s_ce, s_cp = sem("cmp_scores"), sem("cmp_biased"), sem("cmp_exp"), sem("cmp_probs")
    s_ct, s_ctc = sem("cmp_transposed"), sem("cmp_t_copied")
    s_as, s_ab, s_ae, s_sc = sem("att_scores"), sem("att_biased"), sem("att_exp"), sem("att_scaled")
    s_at, s_atc, s_av = sem("att_transposed"), sem("att_t_copied"), sem("att_out")
    s_aoh, s_aol = sem("att_out_hi"), sem("att_out_lo")
    s_hgx, s_hgh, s_hgl = sem("gained"), sem("gained_hi"), sem("gained_lo")
    s_lg, s_le, s_lex, s_selm, s_rank, s_tab = sem("logits"), sem("logits_shifted"), sem("logits_exp"), sem("chosen"), sem("ranked"), sem("jobs_ready")
    s_sel, s_ga, s_gah, s_gal, s_gs, s_sgc = sem("one_hot"), sem("gathered"), sem("gathered_hi"), sem("gathered_lo"), sem("places"), sem("places_copied")
    s_yc, s_scat, s_fin = sem("y_copied"), sem("scattered"), sem("final_ready")

    def kp(w):
        return w.rearrange("(k p) n -> p k n", p=P)

    w_in, w_o, w_kv, w_q, w_bo = kp(a_w_in[0]), kp(a_w_out[0]), kp(b_w_kv), kp(b_w_q[0]), kp(b_w_out[0])
    w_gu, w_dn = kp(f_w_gu[0]), kp(f_w_down[0])
    slots = []
    QK0 = 0
    slots += [w_in[:, :, c * 256:(c + 1) * 256] for c in range(8)]
    V0 = len(slots)
    for c in range(4):
        slots += [w_in[:, k:k + 4, 2 * D + c * 512:2 * D + (c + 1) * 512] for k in (0, 4)]
    O0 = V0 + 4
    WO0 = len(slots)
    slots += [w_o[:, 2 * k:2 * k + 2, :] for k in range(4)]
    FF0 = len(slots)
    for c in range(5):
        for base in (0, FD):
            slots += [w_gu[:, k:k + 4, base + c * 512:base + (c + 1) * 512] for k in (0, 4)]
    slots += [w_gu[:, :, base + 2560:base + 2816] for base in (0, FD)]
    DN0 = len(slots)
    slots += [w_dn[:, 2 * k:2 * k + 2, :] for k in range(11)]
    KV0 = len(slots)
    KV_ORDER = (0, 1, 2, 4, 3, 5)
    slots += [w_kv[:, :, b * 256:(b + 1) * 256] for b in KV_ORDER]
    W10 = len(slots)
    for c in range(2):
        slots += [kp(b_cmp_w1[c])[:, j:j + 8, :] for j in (0, 8)]
    Q0 = len(slots)
    slots += [w_q[:, :, c * 256:(c + 1) * 256] for c in range(4)]
    BO0 = len(slots)
    slots += [w_bo[:, 2 * k:2 * k + 2, :] for k in range(4)]
    N0 = len(slots)

    e_gu = m_w_gu.rearrange("l e (k p) n -> (l e) p k n", p=P)
    e_dn = m_w_down.rearrange("l e (k p) n -> (l e) p k n", p=P)

    def job_slot(e, s):
        if s < 28:
            c, part = divmod(s, 4)
            col = (part // 2) * FE + c * 512
            k0 = (part % 2) * 4
            v = e_gu[e, :, k0:k0 + 4, col:col + 512]
        else:
            k0 = 2 * (s - 28)
            v = e_dn[e, :, k0:k0 + 2, :]
        return v.rearrange("e p k n -> p (e k) n")

    def weights(buf, n, b):
        ring = {id(raw): RAW}.get(id(buf), SPLIT)
        return buf[:, n % ring, :].rearrange("p (a b) -> p a b", b=b)

    def tile_ready(engine, sem_, c, t, n):
        if t == 0:
            engine.wait_ge(sem_, c + 1)
        else:
            engine.wait_ge(s_used, n + 1)

    block = ctx.enter_context(nc.Block())

    @block.sync
    def _(sp):
        def load(n, src, base=0, off=0):
            if base or n >= RAW:
                sp.wait_ge(s_lo, off + n - RAW + 1)
            sp.dma_start(weights(raw, n, src.shape[2]), src).then_inc(landed[n % RAW], 16)

        sp.dma_start(xs[:, 0, :], x[0, 0:P, :]).then_inc(s_x, 16)
        sp.dma_start(xs[:, 1, :], x[0, P:T, :]).then_inc(s_x, 16)
        for n in range(N0):
            load(n, slots[n])
        with sp.Fori(0, NE) as i:
            for s in range(JOB_SLOTS):
                load(N0 + s, job_slot(bass.ds(i, 1), s), 1, i * JOB_SLOTS)
        sp.wait_ge(s_tab, 1)
        jobs = sp.value_load(tab[0:1, 0:1], min_val=NE, max_val=NJ_MAX)
        with sp.If(jobs > NE):
            with sp.Fori(NE, jobs) as i:
                e = sp.value_load(tab[0:1, bass.ds(i - (NE - 1), 1)], min_val=0, max_val=NE - 1)
                for s in range(JOB_SLOTS):
                    load(N0 + s, job_slot(bass.ds(e, 1), s), 1, i * JOB_SLOTS)
        for s in range(AHEAD):
            load(N0 + s, job_slot(slice(0, 1), s), 1, jobs * JOB_SLOTS)
        for t in range(NT):
            sp.wait_ge(s_fin, t + 1)
            sp.dma_start(out[0, t * P:(t + 1) * P, :], xn[:, t, :]).then_inc(s_out, 16)
        sp.wait_ge(s_out, 16 * NT)

    @block.gpsimd
    def _(pool):
        n = [0]
        g = nc.gpsimd

        def step(ins):
            n[0] += 1
            ins.then_inc(s_pc, 1)
            pool.wait_ge(s_pc, n[0])

        step(g.memset(ident[:], 0.0))
        step(g.affine_select(out=ident[:], in_=ident[:], compare_op=ALU.not_equal, fill=1.0, base=0,
                             pattern=[[-1, P]], channel_multiplier=1))
        step(g.memset(consts[:, 0:1], -0.5))
        step(g.memset(consts[:, 1:2], 1.0))
        step(g.memset(consts[:, 2:3], 0.0))
        step(g.memset(ones[:], 1.0))
        step(g.memset(nsel[:], 0.0))
        step(g.affine_select(out=nsel[:], in_=nsel[:], compare_op=ALU.not_equal, fill=-1.0, base=0,
                             pattern=[[-1, HA], [0, P]], channel_multiplier=1))
        step(g.memset(tri_mask[:], 0.0))
        step(g.affine_select(out=tri_mask[:, 0:P], in_=tri_mask[:, 0:P], compare_op=ALU.is_ge, fill=NEG,
                             base=0, pattern=[[1, P]], channel_multiplier=-1))
        g.memset(va[:, :, :, DA:DA + 1], 1.0).then_inc(s_const, 1)

        rr = [0]

        def rstd(m, scale, dst, src):
            pool.wait_ge(m[0], m[1])
            step(g.tensor_scalar(dst, src, scale, EPS, ALU.mult, ALU.add))
            w = dst.shape[1]
            rr[0] += 1
            return g.tensor_tensor(dst, dst, consts[:, 0:1].broadcast_to([P, w]), ALU.pow)

        def norm_rstd(i):
            for t in range(NT):
                rstd((s_sq, NT * i + t + 1), 1.0 / D, stats[:, 2 + 4 * i + t:3 + 4 * i + t],
                     stats[:, 4 * i + t:4 * i + t + 1]).then_inc(s_rstd, 1)

        norm_rstd(0)
        for t in range(NT):
            step(g.iota(cval[:, t, :], [[CS, NC_]], base=CL - 1 - t * P, channel_multiplier=-1,
                        allow_small_or_imprecise_dtypes=True))
            step(g.affine_select(out=cval[:, t, :], in_=cval[:, t, :], compare_op=ALU.is_ge, fill=NEG,
                                 base=t * P - (CL - 1), pattern=[[-CS, NC_]], channel_multiplier=1))
            for h in range(HB):
                step(g.tensor_scalar(dcb[:, t, h, :], cval[:, t, :], float(2.0 ** (-8.0 * (h + 1) / HB)), None, ALU.mult))
            step(g.memset(cval[:, t, :], 1.0))
            step(g.affine_select(out=cval[:, t, :], in_=cval[:, t, :], compare_op=ALU.is_ge, fill=0.0,
                                 base=t * P - (CL - 1), pattern=[[-CS, NC_]], channel_multiplier=1))
        step(g.memset(tri1[:], 1.0))
        step(g.affine_select(out=tri1[:], in_=tri1[:], compare_op=ALU.is_gt, fill=0.0, base=0,
                             pattern=[[1, P]], channel_multiplier=-1))
        step(g.memset(tri8[:], 1.0))
        step(g.affine_select(out=tri8[:], in_=tri8[:], compare_op=ALU.is_gt, fill=0.0, base=0,
                             pattern=[[1, NE], [-1, NE]], channel_multiplier=0))
        step(g.iota(slot_iota[:], [[1, P]], base=0, channel_multiplier=0, allow_small_or_imprecise_dtypes=True))
        g.iota(iot[:], [[1, NE]], base=0, channel_multiplier=0, allow_small_or_imprecise_dtypes=True).then_inc(s_const, 1)
        for b in range(2):
            rstd((s_hq, 4 * (b + 1)), 1.0 / DA, stats[:, 44 + 4 * b:48 + 4 * b], stats[:, 36 + 4 * b:40 + 4 * b]).then_inc(s_hr, 1)
        norm_rstd(1)
        norm_rstd(2)
        pool.wait_ge(s_xu, 8)
        for t in range(NT):
            step(g.iota(dat[:, t, :], [[1, T]], base=-t * P, channel_multiplier=-1, allow_small_or_imprecise_dtypes=True))
            step(g.affine_select(out=dat[:, t, :], in_=dat[:, t, :], compare_op=ALU.is_ge, fill=NEG,
                                 base=t * P, pattern=[[-1, T]], channel_multiplier=1))
        step(g.memset(xf[:, XW - 12:XW], 0.0))
        g.memset(vbd[:], 0.0).then_inc(s_const, 1)
        pool.wait_ge(s_hidt, 1)
        g.memset(pc[:], 0.0).then_inc(s_const, 1)
        norm_rstd(3)
        norm_rstd(4)

    @block.scalar
    def _(act):
        a = nc.scalar.activation
        act.dma_start(pk[:], packed).then_inc(s_pk, 16)
        done = [0]

        def split_to(m):
            while done[0] <= min(m, N0 - 1 + AHEAD):
                n = done[0]
                act.wait_ge(landed[n % RAW], 16 * (n // RAW + 1))
                if n >= SPLIT:
                    act.wait_ge(s_used, n - SPLIT + 1)
                a(w_hi[:, n % SPLIT, :], raw[:, n % RAW, :], ACT.Copy).then_inc(s_hi, 1)
                done[0] += 1

        def squares(i, updates=None):
            for t in range(NT):
                if updates is not None:
                    act.wait_ge(s_xu, updates + 2 * (t + 1))
                else:
                    act.wait_ge(s_x, 16 * NT)
                a(xn[:, t, :], xs[:, t, :], ACT.Square, accum_out=stats[:, 4 * i + t:4 * i + t + 1]).then_inc(s_sq, 1)

        def ht_high(p, gain, banks=(0, 1, 2, 3)):
            for b in range(4):
                act.wait_ge(s_xt, 4 * p + b + 1)
                for k in (2 * b, 2 * b + 1):
                    a(ht_hi[:, k, :], B[banks[b]][:, (k % 2) * 256:(k % 2) * 256 + 256], ACT.Copy,
                      scale=pk[:, C_GAIN + 8 * gain + k:C_GAIN + 8 * gain + k + 1]).then_inc(s_hth, 1)

        squares(0)
        act.wait_ge(s_pk, 16)
        a(ws_hi[:].rearrange("p k n -> p (k n)"), pk[:, C_WS:C_WS + 512], ACT.Copy).then_inc(s_wshi, 1)
        ht_high(0, 0)
        split_to(0)
        act.wait_ge(s_gp, 1)
        a(small[:, 0:16], B[4][:, 0:16], ACT.Copy).then_inc(s_gsb, 1)

        def softplus():
            act.wait_ge(s_lnx, 1)
            a(rows[:, 2, :], rows[:, 2, :], ACT.Exp, scale=-1.0).then_inc(s_ac, 1)
            act.wait_ge(s_ac, 1)
            a(rows[:, 2, :], rows[:, 2, :], ACT.Ln, bias=consts[0:4, 1:2]).then_inc(s_lnd, 1)

        def em_rows():
            act.wait_ge(s_rows, 1)
            a(rows[:, 7, :], rows[:, 6, :], ACT.Exp, scale=-1.0).then_inc(s_rows, 1)
            act.wait_ge(s_cols, 1)
            a(small[:, 16:32], B[5][:, 0:16], ACT.Copy).then_inc(s_colc, 1)

        for s in range(8):
            split_to(s + AHEAD)
            act.wait_ge(s_used, QK0 + s + 1)
            for b in (0, 1):
                blk = 2 * s + b
                a(qk[:, blk, :], B[s % 2][:, b * 256:b * 256 + 256], ACT.Copy,
                  scale=pk[:, C_CONV + 4 * blk + 3:C_CONV + 4 * blk + 4]).then_inc(s_qka, 1)
            if s == 1:
                softplus()
            if s == 3:
                em_rows()
        split_to(V0 + AHEAD)
        for h in range(HA):
            act.wait_ge(s_arg, 2 * h + 2)
            act.wait_ge(s_colc, 1)
            a(wd[:, h, 0:T], wd[:, h, 0:T], ACT.Exp, bias=small[:, 16 + h:17 + h]).then_inc(s_wd, 1)
            a(wd[:, h, T:384], wd[:, h, T:384], ACT.Exp, bias=small[:, 20 + h:21 + h]).then_inc(s_wd, 1)
        for c in range(2):
            split_to(V0 + 2 * c + 1 + AHEAD)
            for t in range(NT):
                tile_ready(act, s_v, c, t, V0 + 2 * c + 1)
                a(va[:, t, 2 * c:2 * c + 2, 0:DA], B[2 + t - 2 * c][:, :].rearrange("p (h d) -> p h d", h=2),
                  ACT.Copy).then_inc(s_vc, 1)

        def o_gate(c):
            for t in range(NT):
                tile_ready(act, s_o, c, t, O0 + 2 * c + 1)
                a(og[:, t, c * 512:(c + 1) * 512], B[2 + t - 2 * c][:, :], ACT.Sigmoid).then_inc(s_oc, 1)

        def head_out(h):
            act.wait_ge(s_den, h + 1)
            for t in range(NT):
                a(xn[:, t, h * DA:(h + 1) * DA], B[6 + t][:, 0:DA], ACT.Copy,
                  scale=stats[:, 52 + t:53 + t]).then_inc(s_hs, 1)
            for t in range(NT):
                act.wait_ge(s_hs, 2 * h + t + 1)
                col = 36 + 4 * (h // 2) + 2 * (h % 2) + t
                a(wd[:, h, 0:DA], xn[:, t, h * DA:(h + 1) * DA], ACT.Square,
                  accum_out=stats[:, col:col + 1]).then_inc(s_hq, 1)
                act.wait_ge(s_hq, 2 * h + t + 1)

        for h in range(HA):
            split_to(O0 + h + AHEAD)
            if h == 3:
                head_out(3)
            if h == 2:
                o_gate(0)
            if h < 3:
                head_out(h)
        split_to(WO0 + AHEAD - 1)
        o_gate(1)
        ht_high(1, 1)
        split_to(FF0 - 1 + AHEAD)
        squares(1, 0)
        ht_high(2, 2)

        def act_high(bank, dst, n):
            act.wait_ge(s_tp, n)
            a(dst, bank, ACT.Copy).then_inc(s_tph, 1)

        def dense_high(c):
            for b in range(2 if c < 5 else 1):
                act_high(B[4 + b][:, :], at_hi[:, (4 * c + 2 * b) * T:(4 * c + 2 * b + 2) * T], 2 * c + b + 1)

        for c in range(6):
            n = FF0 + 4 * c
            width = 512 if c < 5 else 256
            split_to(n + (1 if c < 5 else 0) + AHEAD)
            for t in range(NT):
                tile_ready(act, s_g, c, t, n + (1 if c < 5 else 0))
                if c:
                    act.wait_ge(s_mul, 2 * c)
                a(sg[:, t, 0:width], B[t][:, 0:width], ACT.Silu).then_inc(s_silu, 1)
            if c:
                dense_high(c - 1)
            split_to(n + (3 if c < 5 else 1) + AHEAD)
        dense_high(5)
        split_to(KV0 - 1 + AHEAD)
        squares(2, 4)
        ht_high(3, 3)
        for i in range(6):
            split_to(KV0 + i + AHEAD)
            act.wait_ge(s_used, KV0 + i + 1)
            bank = B[4 + i % 2]
            lower = bank[0:64, :].rearrange("p (b t) -> p b t", b=2)
            if i < 2:
                a(ct[0:64, i, 0::2, :], lower, ACT.Copy).then_inc(s_kva, 1)
                a(ct[64:128, i, 0::2, 0:T - 1], lower[:, :, 1:T], ACT.Copy).then_inc(s_kva, 1)
            elif i < 4:
                a(kt[0:64, i - 2, 0::2, :], lower, ACT.Copy).then_inc(s_kva, 1)
                a(kt[64:128, i - 2, 0::2, :], lower, ACT.Copy).then_inc(s_kva, 1)
            else:
                a(vv[:, :, i - 4, :], bank[:, :].rearrange("p (t d) -> p t d", t=2), ACT.Copy).then_inc(s_kva, 2)
        act.wait_ge(s_xf, 2)
        act.wait_ge(s_const, 3)
        a(xc_hi[:], xf[:], ACT.Copy).then_inc(s_xch, 1)
        act.wait_ge(s_used, W10)
        ht_high(4, 4)
        for c in range(2):
            split_to(W10 + 2 * c + 1 + AHEAD)
            act.wait_ge(s_used, W10 + 2 * c + 2)
            a(hid[:, c, :], B[6 + c][0:G * NC_, 0:CH], ACT.Silu).then_inc(s_hid, 1)
        act.wait_ge(s_hidt, 1)
        a(hidt[:].rearrange("p c h n -> p (c h n)"), B[4][:, 0:4 * G * NC_], ACT.Copy).then_inc(s_hidc, 1)
        act.wait_ge(s_w2, 1)
        a(kc[:, 0:G * NC_], B[5][:, 0:G * NC_], ACT.Copy).then_inc(s_kc, 1)
        for r in range(R):
            a(vbd[32 * r:32 * r + NC_, :, r * DB:(r + 1) * DB],
              B[6][0:NC_, 0:G * DB].rearrange("p (g d) -> p g d", g=G), ACT.Copy).then_inc(s_kc, 1)
        for i in range(4):
            split_to(Q0 + i + AHEAD)
            act.wait_ge(s_used, Q0 + i + 1)
            a(qt[:, 2 * i:2 * i + 2, :], B[i % 2][:, :].rearrange("p (b t) -> p b t", b=2), ACT.Copy,
              scale=DB ** -0.5).then_inc(s_qc, 1)
        act.wait_ge(s_ngb, 1)
        a(gat[:].rearrange("p t n -> p (t n)"), gat[:].rearrange("p t n -> p (t n)"), ACT.Exp, scale=-1.0).then_inc(s_nge, 1)

        def cmp_exp(t):
            act.wait_ge(s_cb, t + 1)
            a(pc[:, :, 0:NC_], pc[:, :, 0:NC_], ACT.Exp).then_inc(s_ce, 1)

        def cmp_t(t):
            act.wait_ge(s_ct, t + 1)
            if t:
                act.wait_ge(s_av, G)
            a(pct[:], B[7][:, :], ACT.Copy).then_inc(s_ctc, 1)

        def head_exp(n):
            lk = P * (n // HB + 1)
            act.wait_ge(s_ab, n + 1)
            for b in range(2):
                v = sc[:, n % 3, b * lk:(b + 1) * lk]
                a(v, v, ACT.Exp, bias=att[:, 0, b, n:n + 1], accum_out=att[:, 1, b, n:n + 1]).then_inc(s_ae, 1)

        def head_t(n):
            blocks = 2 * (n // HB + 1)
            act.wait_ge(s_at, n + 1)
            grp = n // R
            if grp >= 2:
                act.wait_ge(s_av, grp - 1)
            a(ptg[grp % 2][:, 0:blocks, n % R, :], B[(3, 6)[n % 2]][:, 0:blocks * P].rearrange("p (b q) -> p b q", b=blocks),
              ACT.Copy).then_inc(s_atc, 1)

        def group_high(grp):
            t, g = divmod(grp, G)
            act.wait_ge(s_av, grp + 1)
            for odd in range(2):
                a(ht_hi[64 * odd:64 * odd + 64, 2 * g:2 * g + 2, t * P:(t + 1) * P],
                  B[4 + grp % 2][0:64, :].rearrange("p (k o q) -> p o k q", k=2, o=2)[:, odd, :, :],
                  ACT.Copy).then_inc(s_aoh, 1)

        for n in range(2 * HB):
            t, h = divmod(n, HB)
            head_exp(n)
            if h == 1:
                cmp_exp(t)
            if n:
                head_t(n - 1)
            if h == 2:
                cmp_t(t)
            if n >= 2 * R and n % R == 0:
                group_high(n // R - 2)
        head_t(2 * HB - 1)
        group_high(2 * G - 2)
        act.dma_start(gfb[:], norm_final.partition_broadcast(P).rearrange("p a d -> p (a d)")).then_inc(s_gfb, 16)
        group_high(2 * G - 1)
        act.dma_start(g1b[:], norm_ffn1.partition_broadcast(P).rearrange("p a d -> p (a d)")).then_inc(s_g1b, 16)
        split_to(N0 - 1 + AHEAD)
        squares(3, 8)
        ht_high(5, 6)
        for t in range(NT):
            act.wait_ge(s_hgx, t + 1)
            a(hg_hi[:, t, :], xn[:, t, :], ACT.Copy).then_inc(s_hgh, 1)
        act.wait_ge(s_le, 1)
        a(rt[:, 2, :], rt[:, 1, :], ACT.Exp).then_inc(s_lex, 1)
        for h in range(2):
            act.wait_ge(s_ga, h + 1)
            a(ht_hi[:, 2 * h:2 * h + 2, :].rearrange("p k t -> p (k t)"), B[4 + h][:, :], ACT.Copy).then_inc(s_gah, 1)
        act.wait_ge(s_tab, 1)
        jobs = act.value_load(tab[0:1, 0:1], min_val=NE, max_val=NJ_MAX)
        with act.Fori(0, jobs) as i:
            nxt = [AHEAD]

            def split(m):
                while nxt[0] <= m:
                    n = N0 + nxt[0]
                    act.wait_ge(landed[n % RAW], i * (16 * JOB_SLOTS // RAW) + 16 * (n // RAW + 1))
                    act.wait_ge(s_used, i * JOB_SLOTS + n - SPLIT + 1)
                    a(w_hi[:, n % SPLIT, :], raw[:, n % RAW, :], ACT.Copy).then_inc(s_hi, 1)
                    nxt[0] += 1

            def job_high(c):
                act.wait_ge(s_tp, i * 7 + 11 + c + 1)
                a(at_hi[:, 4 * c * P:(4 * c + 4) * P], B[4 + c % 2][:, :], ACT.Copy).then_inc(s_tph, 1)

            act.wait_ge(s_gs, i + 1)
            act.wait_ge(s_xu, i * 4 + 12)
            a(selt[:], B[6][:, 0:2 * P + 1], ACT.Copy).then_inc(s_sgc, 1)
            for c in range(7):
                split(4 * c + 1 + AHEAD)
                act.wait_ge(s_used, i * JOB_SLOTS + N0 + 4 * c + 2)
                act.wait_ge(s_mul, i * 7 + 12 + c)
                a(sg[:, 0, :], B[0][:, :], ACT.Silu).then_inc(s_silu, 1)
                if c:
                    job_high(c - 1)
                split(4 * c + 3 + AHEAD)
            job_high(6)
            split(28 + 2 + AHEAD)
            for h in range(2):
                act.wait_ge(s_ga, i * 2 + 2 + h + 1)
                a(ht_hi[:, 2 * h:2 * h + 2, :].rearrange("p k t -> p (k t)"), B[4 + h][:, :], ACT.Copy).then_inc(s_gah, 1)
            split(JOB_SLOTS - 1 + AHEAD)
            for h in range(2):
                if h == 0:
                    act.wait_ge(s_y, i + 10)
                else:
                    act.wait_ge(s_used, (i + 1) * JOB_SLOTS + N0)
                a(ysb[:, h * 512:(h + 1) * 512], B[2 + h][:, :], ACT.Copy).then_inc(s_yc, 1)
        squares(4, jobs * 4 + 8)


    @block.vector
    def _(dve):
        v = nc.vector
        done, ch = [0], [0]

        def split_to(m):
            while done[0] <= min(m, N0 - 1 + AHEAD):
                n = done[0]
                dve.wait_ge(s_hi, n + 1)
                v.tensor_tensor(w_lo[:, n % SPLIT, :], raw[:, n % RAW, :], w_hi[:, n % SPLIT, :].bitcast(F32),
                                ALU.subtract).then_inc(s_lo, 1)
                done[0] += 1

        def step(ins):
            ch[0] += 1
            ins.then_inc(s_dc, 1)
            dve.wait_ge(s_dc, ch[0])

        def normed(i):
            for t in range(NT):
                dve.wait_ge(s_rstd, NT * i + t + 1)
                v.tensor_scalar(xn[:, t, :], xs[:, t, :], stats[:, 4 * i + 2 + t:4 * i + 3 + t], None,
                                ALU.mult).then_inc(s_xn, 1)

        def ht_low(p, gain, banks=(0, 1, 2, 3)):
            for b in range(4):
                dve.wait_ge(s_hth, 8 * p + 2 * b + 2)
                for k in (2 * b, 2 * b + 1):
                    v.scalar_tensor_tensor(ht_lo[:, k, :], B[banks[b]][:, (k % 2) * 256:(k % 2) * 256 + 256],
                                           pk[:, C_GAIN + 8 * gain + k:C_GAIN + 8 * gain + k + 1],
                                           ht_hi[:, k, :].bitcast(F32), ALU.mult, ALU.subtract).then_inc(s_htl, 1)

        def residual(stage, banks, last_slot):
            for n, b in enumerate(banks):
                t, half = divmod(n, 2)
                if n < 3:
                    dve.wait_ge(s_y, 3 * stage + n + 1)
                else:
                    dve.wait_ge(s_used, last_slot + 1)
                xv = xs[:, t, half * 512:(half + 1) * 512]
                v.tensor_tensor(xv, xv, B[b][:, :], ALU.add).then_inc(s_xu, 1)

        normed(0)
        dve.wait_ge(s_wshi, 1)
        v.tensor_tensor(ws_lo[:].rearrange("p k n -> p (k n)"), pk[:, C_WS:C_WS + 512],
                        ws_hi[:].rearrange("p k n -> p (k n)").bitcast(F32), ALU.subtract).then_inc(s_wslo, 1)
        ht_low(0, 0)

        def gate_rows():
            dve.wait_ge(s_grow, 1)
            step(v.tensor_scalar(rows[:, 0, :], B[4][0:4, 0:T], pk[0:4, C_BIF:C_BIF + 1], None, ALU.add))
            step(v.tensor_scalar(rows[:, 1, :], B[4][0:4, T:2 * T], pk[0:4, C_BIF + 1:C_BIF + 2], None, ALU.add))
            v.scalar_tensor_tensor(rows[:, 2, :], rows[:, 1, :], -1.0, rows[:, 1, :], ALU.mult, ALU.max).then_inc(s_lnx, 1)
            dve.wait_ge(s_lnx, 1)
            step(v.tensor_scalar(rows[:, 1, :], rows[:, 1, :], 0.0, None, ALU.min))

        def gate_scans():
            dve.wait_ge(s_lnd, 1)
            step(v.tensor_tensor(rows[:, 1, :], rows[:, 1, :], rows[:, 2, :], ALU.subtract))
            step(v.tensor_tensor_scan(rows[:, 3, :], ones[0:4, 0:1].broadcast_to([4, T]), rows[:, 1, :], 0.0,
                                      ALU.mult, ALU.add))
            step(v.tensor_tensor(rows[:, 4, :], rows[:, 0, :], rows[:, 3, :], ALU.subtract))
            step(v.tensor_tensor_scan(rows[:, 5, :], rows[:, 4, :], rows[:, 4, :], 0.0, ALU.max, ALU.max))
            v.tensor_tensor(rows[:, 6, :], rows[:, 3, :], rows[:, 5, :], ALU.add).then_inc(s_rows, 1)

        for s in range(8):
            split_to(s + AHEAD)
            dve.wait_ge(s_qka, 2 * s + 2)
            for j in (1, 2, 3):
                for b in (0, 1):
                    blk = 2 * s + b
                    if j > 1:
                        dve.wait_ge(s_dc, ch[0] - 1)
                    ins = v.scalar_tensor_tensor(
                        qk[:, blk, j:T], B[s % 2][:, b * 256:b * 256 + T - j],
                        pk[:, C_CONV + 4 * blk + 3 - j:C_CONV + 4 * blk + 4 - j], qk[:, blk, j:T], ALU.mult, ALU.add)
                    if j < 3 or b == 0:
                        ch[0] += 1
                        ins.then_inc(s_dc, 1)
            ins.then_inc(s_conv, 1)
            if s == 1:
                gate_rows()
            if s == 2:
                gate_scans()
        split_to(V0 + AHEAD - 1)
        for h in range(HA):
            dve.wait_ge(s_nm, 1)
            src = B[6 + h // 2][:, (h % 2) * T:(h % 2) * T + T]
            v.tensor_tensor(wd[:, h, 0:T], src, tri_mask[:, :], ALU.add).then_inc(s_arg, 1)
            v.tensor_tensor(wd[:, h, T:384], src[:, P:T], tri_mask[:, 0:P], ALU.add).then_inc(s_arg, 1)
        split_to(O0 + AHEAD - 1)

        def weighted(h):
            dve.wait_ge(s_s, h + 1)
            dve.wait_ge(s_wd, 2 * h + 2)
            if h >= 2:
                dve.wait_ge(s_num, h - 1)
            v.scalar_tensor_tensor(pd[:, h % 2, :], B[4 + h % 2][:, 0:384], DA ** -0.5, wd[:, h, :],
                                   ALU.mult, ALU.mult).then_inc(s_p, 1)

        def inv_den(h):
            dve.wait_ge(s_num, h + 1)
            for t in range(NT):
                if h:
                    dve.wait_ge(s_hs, 2 * h)
                den, lim = B[6 + t][:, DA:DA + 1], small[:, 24 + 4 * t + h:25 + 4 * t + h]
                size = stats[:, 54 + t:55 + t]
                step(v.scalar_tensor_tensor(size, den, -1.0, lim, ALU.mult, ALU.max))
                step(v.tensor_tensor(size, size, den, ALU.max))
            v.reciprocal(stats[:, 52:54], stats[:, 54:56]).then_inc(s_den, 1)

        weighted(0)
        for h in range(HA):
            if h + 1 < HA:
                weighted(h + 1)
            if h < 3:
                split_to(O0 + h + AHEAD)
            inv_den(h)
        split_to(WO0 + AHEAD - 1)
        for b in range(2):
            dve.wait_ge(s_hr, b + 1)
            dve.wait_ge(s_oc, 2 * b + 2)
            for t in range(NT):
                for h in (2 * b, 2 * b + 1):
                    xv = xn[:, t, h * DA:(h + 1) * DA]
                    col = 44 + 4 * b + 2 * (h % 2) + t
                    ins = v.scalar_tensor_tensor(xv, xv, stats[:, col:col + 1], og[:, t, h * DA:(h + 1) * DA],
                                                 ALU.mult, ALU.mult)
                    if h == 3:
                        dve.wait_ge(s_dc, ch[0])
                        ins.then_inc(s_xn, 1)
                    else:
                        ins.then_inc(s_dc, 1)
                        ch[0] += 1
        ht_low(1, 1)
        split_to(FF0 - 1 + AHEAD)
        residual(0, (4, 5, 6, 7), FF0 - 1)
        normed(1)
        ht_low(2, 2)

        def dense_low(c):
            for b in range(2 if c < 5 else 1):
                dve.wait_ge(s_tph, 2 * c + b + 1)
                dst = slice((4 * c + 2 * b) * T, (4 * c + 2 * b + 2) * T)
                v.tensor_tensor(at_lo[:, dst], B[4 + b][:, :], at_hi[:, dst].bitcast(F32), ALU.subtract).then_inc(s_tpl, 1)

        for c in range(6):
            n = FF0 + 4 * c
            width = 512 if c < 5 else 256
            split_to(n + (1 if c < 5 else 0) + AHEAD)
            if c:
                dense_low(c - 1)
            split_to(n + (3 if c < 5 else 1) + AHEAD)
            for t in range(NT):
                tile_ready(dve, s_u, c, t, n + (3 if c < 5 else 1))
                dve.wait_ge(s_silu, 2 * c + t + 1)
                if c:
                    dve.wait_ge(s_tp, 2 * c)
                v.tensor_tensor(av[:, t, 0:width], sg[:, t, 0:width], B[2 + t][:, 0:width], ALU.mult).then_inc(s_mul, 1)
        dense_low(5)
        split_to(KV0 - 1 + AHEAD)
        residual(1, (0, 1, 2, 3), KV0 - 1)
        normed(2)
        ht_low(3, 3)
        for i in range(6):
            split_to(KV0 + i + AHEAD)
            if i < 4:
                dve.wait_ge(s_used, KV0 + i + 1)
                upper = B[4 + i % 2][64:128, :].rearrange("p (b t) -> p b t", b=2)
                if i < 2:
                    v.tensor_copy(ct[0:64, i, 1::2, :], upper).then_inc(s_kvd, 1)
                    v.tensor_copy(ct[64:128, i, 1::2, 0:T - 1], upper[:, :, 1:T]).then_inc(s_kvd, 1)
                else:
                    v.tensor_copy(kt[0:64, i - 2, 1::2, :], upper).then_inc(s_kvd, 1)
                    v.tensor_copy(kt[64:128, i - 2, 1::2, :], upper).then_inc(s_kvd, 1)
        for c in range(2):
            dve.wait_ge(s_kva, 2 * c + 2)
            dve.wait_ge(s_kvd, 2 * c + 2)
            dst = xf[:, 960 * c:960 * c + 960].rearrange("p (j n) -> p j n", j=16)
            for g in range(G):
                src = ct[:, c, g, :]
                blocks = bass.AP(src.tensor, src.offset, [list(src.ap[0]), [2, 16], [CS, NC_]])
                pos = pk[:, C_POS + 16 * c:C_POS + 16 * c + 16].rearrange("p (j o) -> p j o", o=1).broadcast_to([P, 16, NC_])
                ins = v.tensor_tensor(dst[:, :, g * NC_:(g + 1) * NC_], blocks, pos, ALU.add)
                if g == G - 1:
                    dve.wait_ge(s_dc, ch[0])
                    ins.then_inc(s_xf, 1)
                else:
                    ins.then_inc(s_dc, 1)
                    ch[0] += 1
        dve.wait_ge(s_xch, 1)
        v.tensor_tensor(xc_lo[:], xf[:], xc_hi[:].bitcast(F32), ALU.subtract).then_inc(s_xf, 1)
        ht_low(4, 4)
        split_to(Q0 + 3 + AHEAD)
        dve.wait_ge(s_ng, 1)
        v.tensor_tensor(gat[:], B[2][:, 0:96].rearrange("p (t n) -> p t n", t=2),
                        pk[:, C_BG:C_BG + 48].rearrange("p (o n) -> p o n", o=1).broadcast_to([P, 2, 48]),
                        ALU.add).then_inc(s_ngb, 1)
        dve.wait_ge(s_nge, 1)
        g96 = gat[:].rearrange("p t n -> p (t n)")
        step(v.tensor_scalar(g96, g96, 1.0, None, ALU.add))
        step(v.reciprocal(g96, g96))

        def cmp_bias(t):
            dve.wait_ge(s_cs, 2 * t + 2)
            if t:
                dve.wait_ge(s_ct, t)
            p = pc[:, :, 0:NC_]
            step(v.tensor_tensor(p, B[7][:, :].rearrange("p (h n) -> p h n", n=32)[:, :, 0:NC_], dcb[:, t, :, :], ALU.add))
            step(v.tensor_reduce(cmx[:, 0, :], p, AX.X, ALU.max))
            v.tensor_tensor(p, p, cmx[:, 0, :].rearrange("p (h o) -> p h o", o=1).broadcast_to([P, HB, NC_]),
                            ALU.subtract).then_inc(s_cb, 1)

        def cmp_probs(t):
            dve.wait_ge(s_ce, t + 1)
            p = pc[:, :, 0:NC_]
            step(v.tensor_tensor(p, p, cval[:, t, :].rearrange("p (o n) -> p o n", o=1).broadcast_to([P, HB, NC_]),
                                 ALU.mult))
            step(v.tensor_reduce(cmx[:, 1, :], p, AX.X, ALU.add))
            step(v.tensor_scalar(cmx[:, 1, :], cmx[:, 1, :], 1e-30, None, ALU.max))
            step(v.reciprocal(cmx[:, 1, :], cmx[:, 1, :]))
            gv = gat[:, t, :].rearrange("p (h b) -> p h b", b=3)
            step(v.tensor_tensor(cmx[:, 1, :], cmx[:, 1, :], gv[:, :, 0], ALU.mult))
            v.tensor_tensor(p, p, cmx[:, 1, :].rearrange("p (h o) -> p h o", o=1).broadcast_to([P, HB, NC_]),
                            ALU.mult).then_inc(s_cp, 1)

        def head_bias(n):
            t, h = divmod(n, HB)
            lk = P * (t + 1)
            dve.wait_ge(s_as, n + 1)
            if n >= 3:
                dve.wait_ge(s_at, n - 2)
            dst = sc[:, n % 3, 0:2 * lk].rearrange("p (b k) -> p b k", b=2)
            step(v.scalar_tensor_tensor(
                dst, dat[:, t, 0:lk].rearrange("p (o k) -> p o k", o=1).broadcast_to([P, 2, lk]),
                float(2.0 ** (-8.0 * (h + 1) / HB)), B[n % 3][:, 0:2 * lk].rearrange("p (b k) -> p b k", b=2),
                ALU.mult, ALU.add))
            v.tensor_reduce(att[:, 0, :, n:n + 1], dst, AX.X, ALU.max, negate=True).then_inc(s_ab, 1)

        def head_scale(n):
            t, h = divmod(n, HB)
            lk = P * (t + 1)
            dve.wait_ge(s_ae, 2 * n + 2)
            step(v.reciprocal(coef[:, :, n:n + 1], att[:, 1, :, n:n + 1]))
            step(v.tensor_tensor(coef[:, :, n:n + 1], coef[:, :, n:n + 1],
                                 gat[:, t, 3 * h + 1:3 * h + 3].rearrange("p (b o) -> p b o", o=1), ALU.mult))
            for b in range(2):
                vv_ = sc[:, n % 3, b * lk:(b + 1) * lk]
                v.tensor_scalar(vv_, vv_, coef[:, b, n:n + 1], None, ALU.mult).then_inc(s_sc, 1)

        def group_low(grp):
            t, g = divmod(grp, G)
            dve.wait_ge(s_aoh, 2 * grp + 2)
            for odd in range(2):
                dst = (slice(64 * odd, 64 * odd + 64), slice(2 * g, 2 * g + 2), slice(t * P, (t + 1) * P))
                v.tensor_tensor(ht_lo[dst], B[4 + grp % 2][0:64, :].rearrange("p (k o q) -> p o k q", k=2, o=2)[:, odd, :, :],
                                ht_hi[dst].bitcast(F32), ALU.subtract).then_inc(s_aol, 1)

        dve.wait_ge(s_const, 4)
        head_bias(0)
        for n in range(2 * HB):
            t, h = divmod(n, HB)
            if n + 1 < 2 * HB:
                head_bias(n + 1)
            if h == 0:
                cmp_bias(t)
            head_scale(n)
            if h == 1:
                cmp_probs(t)
            if n >= 2 * R and n % R == 0:
                group_low(n // R - 2)
        group_low(2 * G - 2)
        group_low(2 * G - 1)
        split_to(N0 - 1 + AHEAD)
        residual(2, (4, 5, 6, 7), N0 - 1)
        normed(3)
        ht_low(5, 6)
        dve.wait_ge(s_xt, 24)
        dve.wait_ge(s_g1b, 16)
        for t in range(NT):
            v.tensor_tensor(xn[:, t, :], xn[:, t, :], g1b[:], ALU.mult).then_inc(s_hgx, 1)
        for t in range(NT):
            dve.wait_ge(s_hgh, t + 1)
            v.tensor_tensor(hg_lo[:, t, :], xn[:, t, :], hg_hi[:, t, :].bitcast(F32), ALU.subtract).then_inc(s_hgl, 1)
        def one_hot(j):
            for t in range(NT):
                v.tensor_tensor(sel_oh[:, t, :], slot_iota[:], posj[:, t, j].broadcast_to([P, P]),
                                ALU.is_equal).then_inc(s_sel, 1)

        r = [rt[:, k, :].rearrange("p (t e) -> p t e", t=NT) for k in range(16)]
        rf = [rt[:, k, :] for k in range(16)]
        L = r[0]
        dve.wait_ge(s_lg, 1)
        step(v.tensor_copy(L, B[0][:, 0:NT * NE].rearrange("p (t e) -> p t e", t=NT)))
        wins = big8[:, 0, :].rearrange("p (t e f) -> p t e f", t=NT, e=NE)
        ties = big8[:, 1, :].rearrange("p (t e f) -> p t e f", t=NT, e=NE)
        for t in range(NT):
            mine = L[:, t, :].rearrange("p (e o) -> p e o", o=1).broadcast_to([P, NE, NE])
            other = L[:, t, :].rearrange("p (o e) -> p o e", o=1).broadcast_to([P, NE, NE])
            v.tensor_tensor(wins[:, t, :, :], other, mine, ALU.is_gt).then_inc(s_dc, 1)
            v.tensor_tensor(ties[:, t, :, :], other, mine, ALU.is_equal).then_inc(s_dc, 1)
            ch[0] += 2
        step(v.tensor_reduce(r[4][:, :, 0], L, AX.X, ALU.max))
        v.tensor_tensor(r[1], L, r[4][:, :, 0:1].broadcast_to([P, NT, NE]), ALU.subtract).then_inc(s_le, 1)
        step(v.tensor_tensor(ties, ties, tri8[:].rearrange("p (o e) f -> p o e f", o=1).broadcast_to([P, NT, NE, NE]), ALU.mult))
        step(v.tensor_tensor(wins, wins, ties, ALU.add))
        step(v.tensor_reduce(r[3], wins, AX.X, ALU.add))
        v.tensor_scalar(rf[5], rf[3], 2.0, None, ALU.is_lt).then_inc(s_selm, 1)
        dve.wait_ge(s_selm, 1)
        dve.wait_ge(s_lex, 1)
        step(v.tensor_tensor(rf[2], rf[2], rf[5], ALU.mult))
        step(v.tensor_reduce(r[4][:, :, 1], r[2], AX.X, ALU.add))
        step(v.reciprocal(r[4][:, :, 2], r[4][:, :, 1]))
        step(v.tensor_tensor(gatej[:, :, 0:NE], r[2], r[4][:, :, 2:3].broadcast_to([P, NT, NE]), ALU.mult))
        dve.wait_ge(s_rank, 1)
        cnt = r[7][:, 0, :]
        step(v.tensor_copy(r[6], B[1][:, 0:NT * NE].rearrange("p (t e) -> p t e", t=NT)))
        step(v.tensor_copy(cnt, B[1][:, NT * NE:NT * NE + NE]))
        step(v.scalar_tensor_tensor(rf[6], rf[6], 1.0, rf[5], ALU.add, ALU.mult))
        step(v.tensor_scalar(posj[:, :, 0:NE], r[6], -1.0, None, ALU.add))
        one_hot(slice(0, 1))
        over, rank = r[8][:, 0, :], r[8][:, 1, :]
        v.memset(posj[:, :, NJ_MAX:12], -1.0).then_inc(s_dc, 1)
        v.memset(gatej[:, :, NJ_MAX:12], 0.0).then_inc(s_dc, 1)
        v.memset(rf[15], 0.0).then_inc(s_dc, 1)
        ch[0] += 3
        step(v.tensor_scalar(over, cnt, float(P), None, ALU.is_gt))
        step(v.tensor_tensor_scan(rank, ones[:, 0:NE], over, 0.0, ALU.mult, ALU.add))
        nk = NJ_MAX - NE
        pick = big8[:, 0, 0:nk * NE].rearrange("p (k e) -> p k e", k=nk)
        work = big8[:, 1, 0:NT * nk * NE].rearrange("p (t k e) -> p t k e", t=NT, k=nk)
        num = iot[:, 1:1 + nk].rearrange("p (k o) -> p k o", o=1).broadcast_to([P, nk, NE])

        def over_k(v_):
            return v_.rearrange("p (o e) -> p o e", o=1).broadcast_to([P, nk, NE])

        step(v.tensor_tensor(pick, over_k(rank), num, ALU.is_equal))
        step(v.tensor_tensor(pick, pick, over_k(over), ALU.mult))
        step(v.tensor_tensor(work[:, 0, :, :], pick, over_k(iot[:]), ALU.mult))
        v.tensor_scalar(rf[15][0:1, 0:1], rank[0:1, NE - 1:NE], float(NE), None, ALU.add).then_inc(s_dc, 1)
        ch[0] += 1
        step(v.tensor_reduce(rf[15][0:1, 1:1 + nk], work[0:1, 0, :, :], AX.X, ALU.add))
        pick_t = pick.rearrange("p (o k) e -> p o k e", o=1).broadcast_to([P, NT, nk, NE])
        for table, less in ((posj, -float(P)), (gatej, 0.0)):
            step(v.tensor_tensor(work, pick_t, table[:, :, 0:NE].rearrange("p t (o e) -> p t o e", o=1)
                                 .broadcast_to([P, NT, nk, NE]), ALU.mult))
            dst = table[:, :, NE:NJ_MAX]
            step(v.tensor_reduce(dst, work, AX.X, ALU.add))
            if less:
                step(v.tensor_scalar(dst, dst, less, None, ALU.add))
        v.tensor_copy(tab[0:1, 0:16], rf[15][0:1, 0:16]).then_inc(s_tab, 1)

        def gathered_low(n):
            for h in range(2):
                dve.wait_ge(s_gah, n + h + 1)
                v.tensor_tensor(ht_lo[:, 2 * h:2 * h + 2, :].rearrange("p k t -> p (k t)"), B[4 + h][:, :],
                                ht_hi[:, 2 * h:2 * h + 2, :].rearrange("p k t -> p (k t)").bitcast(F32),
                                ALU.subtract).then_inc(s_gal, 1)

        gathered_low(0)
        dve.wait_ge(s_tab, 1)
        jobs = dve.value_load(tab[0:1, 0:1], min_val=NE, max_val=NJ_MAX)
        with dve.Fori(0, jobs) as i:
            nxt = [AHEAD]

            def split(m):
                while nxt[0] <= m:
                    n = N0 + nxt[0]
                    dve.wait_ge(s_hi, i * JOB_SLOTS + n + 1)
                    v.tensor_tensor(w_lo[:, n % SPLIT, :], raw[:, n % RAW, :], w_hi[:, n % SPLIT, :].bitcast(F32),
                                    ALU.subtract).then_inc(s_lo, 1)
                    nxt[0] += 1

            def job_low(c):
                dve.wait_ge(s_tph, i * 7 + 11 + c + 1)
                dst = slice(4 * c * P, (4 * c + 4) * P)
                v.tensor_tensor(at_lo[:, dst], B[4 + c % 2][:, :], at_hi[:, dst].bitcast(F32), ALU.subtract).then_inc(s_tpl, 1)

            for c in range(7):
                split(4 * c + 1 + AHEAD)
                if c:
                    job_low(c - 1)
                split(4 * c + 3 + AHEAD)
                if c == 0:
                    dve.wait_ge(s_sgc, i + 1)
                dve.wait_ge(s_used, i * JOB_SLOTS + N0 + 4 * c + 4)
                dve.wait_ge(s_silu, i * 7 + 12 + c + 1)
                dve.wait_ge(s_tp, i * 7 + 11 + c)
                v.scalar_tensor_tensor(av[:, 0, :], sg[:, 0, :], selt[:, 2 * P:2 * P + 1], B[1][:, :],
                                       ALU.mult, ALU.mult).then_inc(s_mul, 1)
            dve.wait_ge(s_gs, i + 1)
            one_hot(bass.ds(i + 1, 1))
            job_low(6)
            split(28 + 2 + AHEAD)
            gathered_low(i * 2 + 2)
            split(JOB_SLOTS - 1 + AHEAD)
            for n, b in enumerate((0, 1, 7, 5)):
                t, half = divmod(n, 2)
                dve.wait_ge(s_scat, i * 4 + n + 1)
                dve.wait_ge(s_xu, i * 4 + 9 + n)
                xv = xs[:, t, half * 512:(half + 1) * 512]
                v.tensor_tensor(xv, xv, B[b][:, :], ALU.add).then_inc(s_xu, 1)
        dve.wait_ge(s_gfb, 16)
        for t in range(NT):
            dve.wait_ge(s_rstd, 4 * NT + t + 1)
            v.scalar_tensor_tensor(xn[:, t, :], xs[:, t, :], stats[:, 18 + t:19 + t], gfb[:], ALU.mult,
                                   ALU.mult).then_inc(s_fin, 1)

    @block.tensor
    def _(pe):
        mm = nc.tensor.matmul

        def mm3(out_, sh, sl, mh, ml, first, last):
            mm(out_, sh, mh, start=first, stop=False)
            mm(out_, sh, ml, start=False, stop=False)
            return mm(out_, sl, mh, start=False, stop=last)

        def wait_slot(n, i=None):
            pe.wait_ge(s_lo, (n if i is None else i * JOB_SLOTS + n) + 1)

        def transposed(p, xn_count, banks=(0, 1, 2, 3)):
            for t in range(NT):
                pe.wait_ge(s_xn, xn_count - NT + t + 1)
                for k in range(KD):
                    ins = nc.tensor.transpose(B[banks[k // 2]][:, (k % 2) * 256 + t * P:(k % 2) * 256 + (t + 1) * P],
                                              xn[:, t, k * P:(k + 1) * P], ident[:])
                    if t == NT - 1 and k % 2:
                        ins.then_inc(s_xt, 1)

        def fresh_k(fresh, k):
            if fresh is not None and k % 2 == 0:
                pe.wait_ge(s_htl, 8 * fresh + k + 2)

        def hth(k, t):
            return ht_hi[:, k, t * P:(t + 1) * P]

        def htl(k, t):
            return ht_lo[:, k, t * P:(t + 1) * P]

        def features(n, bank, fresh=None):
            wait_slot(n)
            for b in range(2):
                for k in range(KD):
                    if b == 0:
                        fresh_k(fresh, k)
                    ins = mm3(bank[:, b * 256:b * 256 + 256], weights(w_hi, n, 256)[:, k, b * P:(b + 1) * P],
                              weights(w_lo, n, 256)[:, k, b * P:(b + 1) * P], ht_hi[:, k, :], ht_lo[:, k, :],
                              k == 0, k == KD - 1)
            ins.then_inc(s_used, 1)

        def wide(n, b, banks, kt0, nkt, first, last, sem_, hi=hth, lo=htl, fresh=None):
            wait_slot(n)
            for t in range(NT):
                for k in range(nkt):
                    if t == 0:
                        fresh_k(fresh, kt0 + k)
                    ins = mm3(B[banks[t]][:, 0:b], hi(kt0 + k, t), lo(kt0 + k, t), weights(w_hi, n, b)[:, k, :],
                              weights(w_lo, n, b)[:, k, :], first and k == 0, last and k == nkt - 1)
                if last and t == 0:
                    ins.then_inc(sem_, 1)
            ins.then_inc(s_used, 1)

        def down(n, banks, kt0, first, last, hi=hth, lo=htl, fresh=None):
            wait_slot(n)
            fresh_k(fresh, kt0)
            for t in range(NT):
                for half in range(2):
                    for k in range(2):
                        w = slice(half * 512, half * 512 + 512)
                        ins = mm3(B[banks[2 * t + half]][:, :], hi(kt0 + k, t), lo(kt0 + k, t),
                                  weights(w_hi, n, 1024)[:, k, w], weights(w_lo, n, 1024)[:, k, w],
                                  first and k == 0, last and k == 1)
                    if last and 2 * t + half < 3:
                        ins.then_inc(s_y, 1)
            ins.then_inc(s_used, 1)

        def small_tokens(bank, cols, width, fresh=None):
            for t in range(NT):
                for k in range(KD):
                    if t == 0:
                        fresh_k(fresh, k)
                    ins = mm3(bank[:, t * width:(t + 1) * width], hth(k, t), htl(k, t), ws_hi[:, k, cols],
                              ws_lo[:, k, cols], k == 0, k == KD - 1)
            return ins

        pe.wait_ge(s_const, 1)
        transposed(0, 2)
        pe.wait_ge(s_wslo, 1)
        small_tokens(B[4], slice(0, 8), 8, 0).then_inc(s_gp, 1)
        for s in range(8):
            if s >= 2:
                pe.wait_ge(s_conv, s - 1)
            features(QK0 + s, B[s % 2])
            if s == 0:
                pe.wait_ge(s_gsb, 1)
                for part in range(2):
                    for t in range(NT):
                        ins = nc.tensor.transpose(B[4][0:4, part * T + t * P:part * T + (t + 1) * P],
                                                  small[:, t * 8 + 4 * part:t * 8 + 4 * part + 4], ident[:])
                ins.then_inc(s_grow, 1)
            if s == 4:
                pe.wait_ge(s_rows, 2)
                for row, c0 in ((4, 0), (7, 8)):
                    for t in range(NT):
                        ins = nc.tensor.transpose(B[5][:, c0 + 4 * t:c0 + 4 * t + 4],
                                                  rows[:, row, t * P:(t + 1) * P], ident[0:4, 0:4])
                ins.then_inc(s_cols, 1)
                for h in range(HA):
                    ins = mm(B[6 + h // 2][:, (h % 2) * T:(h % 2) * T + T], nsel[:, h, :], rows[:, 5, :],
                             start=True, stop=True)
                ins.then_inc(s_nm, 1)
        for c in range(2):
            if c == 1:
                pe.wait_ge(s_conv, 8)
            for half in range(2):
                wide(V0 + 2 * c + half, 512, (2 - 2 * c, 3 - 2 * c), 4 * half, 4, half == 0, half == 1, s_v)

        def scores(h):
            if h == 0:
                pe.wait_ge(s_conv, 8)
                pe.wait_ge(s_colc, 1)
            if h >= 2:
                pe.wait_ge(s_p, h - 1)
            bank = B[4 + h % 2]
            for d in range(2):
                mm(bank[:, 0:T], qk[:, 8 + 2 * h + d, 0:P], qk[:, 2 * h + d, :], start=d == 0, stop=d == 1)
            for d in range(2):
                ins = mm(bank[:, T:384], qk[:, 8 + 2 * h + d, P:T], qk[:, 2 * h + d, P:T], start=d == 0, stop=d == 1)
            ins.then_inc(s_s, 1)

        def numerator(h):
            pe.wait_ge(s_p, h + 1)
            pe.wait_ge(s_vc, 4)
            if h == 0:
                pe.wait_ge(s_arg, 8)
            else:
                pe.wait_ge(s_hs, 2 * h)
            p = pd[:, h % 2, :]
            mm(B[6][:, 0:DA + 1], p[:, 0:P], va[:, 0, h, :], start=True, stop=True)
            mm(B[7][:, 0:DA + 1], p[:, P:T], va[:, 0, h, :], start=True, stop=False)
            mm(B[7][:, 0:DA + 1], p[:, T:384], va[:, 1, h, :], start=False, stop=True).then_inc(s_num, 1)

        scores(0)
        scores(1)
        pe.wait_ge(s_vc, 2)
        for h in range(HA):
            if h == 2:
                pe.wait_ge(s_vc, 4)
            c, half = divmod(h, 2)
            if h < 3:
                wide(O0 + h, 512, (2 - 2 * c, 3 - 2 * c), 4 * half, 4, half == 0, half == 1, s_o)
            numerator(h)
            if h + 2 < HA:
                scores(h + 2)
        wide(O0 + 3, 512, (0, 1), 4, 4, False, True, s_o)
        pe.wait_ge(s_oc, 4)
        transposed(1, 4)
        for k in range(4):
            down(WO0 + k, (4, 5, 6, 7), 2 * k, k == 0, k == 3, fresh=1)
        transposed(2, 6)
        def dense_t(c):
            pe.wait_ge(s_mul, 2 * c + 2)
            for b in range(2 if c < 5 else 1):
                if c:
                    pe.wait_ge(s_tpl, 2 * (c - 1) + b + 1)
                for j in range(2):
                    for t in range(NT):
                        blk = 2 * b + j
                        ins = nc.tensor.transpose(B[4 + b][:, j * 256 + t * P:j * 256 + (t + 1) * P],
                                                  av[:, t, blk * P:(blk + 1) * P], ident[:])
                ins.then_inc(s_tp, 1)

        for c in range(6):
            n = FF0 + 4 * c
            if c:
                pe.wait_ge(s_silu, 2 * c)
            else:
                pe.wait_ge(s_htl, 20)
            if c < 5:
                for half in range(2):
                    wide(n + half, 512, (0, 1), 4 * half, 4, half == 0, half == 1, s_g, fresh=None if c else 2)
            else:
                wide(n, 256, (0, 1), 0, 8, True, True, s_g)
            if c:
                dense_t(c - 1)
                pe.wait_ge(s_mul, 2 * c)
            if c < 5:
                for half in range(2):
                    wide(n + 2 + half, 512, (2, 3), 4 * half, 4, half == 0, half == 1, s_u)
            else:
                wide(n + 1, 256, (2, 3), 0, 8, True, True, s_u)
        dense_t(5)

        def ath(k, t):
            return at_hi[:, k * T + t * P:k * T + (t + 1) * P]

        def atl(k, t):
            return at_lo[:, k * T + t * P:k * T + (t + 1) * P]

        pe.wait_ge(s_silu, 12)
        for k in range(11):
            pe.wait_ge(s_tpl, min(k + 1, 11))
            down(DN0 + k, (0, 1, 2, 3), 2 * k, k == 0, k == 10, ath, atl)
        transposed(3, 8)
        for i in range(6):
            if i >= 2:
                pe.wait_ge(s_kva, 2 * (i - 1))
                pe.wait_ge(s_kvd, 2 * (i - 1))
            bank = B[4 + i % 2]
            n = KV0 + i
            if i < 4:
                features(n, bank, None if i else 3)
            else:
                wait_slot(n)
                for t in range(NT):
                    for k in range(KD):
                        ins = mm3(bank[:, t * 256:(t + 1) * 256], hth(k, t), htl(k, t), weights(w_hi, n, 256)[:, k, :],
                                  weights(w_lo, n, 256)[:, k, :], k == 0, k == KD - 1)
                ins.then_inc(s_used, 1)
        transposed(4, 8)
        for c in range(2):
            if c == 0:
                pe.wait_ge(s_xf, 3)
            for half in range(2):
                n = W10 + 2 * c + half
                wait_slot(n)
                for j in range(8):
                    jj = 8 * half + j
                    at = 960 * c + 60 * jj
                    ins = mm3(B[6 + c][0:XM, 0:CH], xc_hi[:, at:at + XM], xc_lo[:, at:at + XM],
                              weights(w_hi, n, CH)[:, j, :], weights(w_lo, n, CH)[:, j, :], jj == 0, jj == 15)
                ins.then_inc(s_used, 1)
        pe.wait_ge(s_hid, 2)
        pe.wait_ge(s_kva, 12)
        for c in range(2):
            for hb in range(2):
                ins = nc.tensor.transpose(B[4][:, (2 * c + hb) * 60:(2 * c + hb) * 60 + 60],
                                          hid[:, c, hb * P:(hb + 1) * P], ident[0:G * NC_, 0:G * NC_])
        ins.then_inc(s_hidt, 1)
        features(Q0, B[0], 4)
        pe.wait_ge(s_hidc, 1)
        w2 = pk[:, C_W2:C_W2 + 256].rearrange("p (c h d) -> p c h d", c=2, h=2)
        for top in (0, 64):
            for hb in range(2):
                mm(B[5][top:top + 64, 0:G * NC_], w2[:, 0, hb, :], hidt[:, 0, hb, :], start=hb == 0, stop=hb == 1)
        for g in range(G):
            for hb in range(2):
                ins = mm(B[6][0:NC_, g * DB:(g + 1) * DB], hidt[:, 1, hb, g * NC_:(g + 1) * NC_], w2[:, 1, hb, :],
                         start=hb == 0, stop=hb == 1)
        ins.then_inc(s_w2, 1)
        for i in range(1, 4):
            if i >= 2:
                pe.wait_ge(s_qc, i - 1)
            features(Q0 + i, B[i % 2])
        small_tokens(B[2], slice(8, 56), 48).then_inc(s_ng, 1)
        pe.wait_ge(s_kc, 5)

        def cmp_scores(t):
            if t:
                pe.wait_ge(s_ctc, t)
            for odd in range(2):
                for h in range(odd, HB, 2):
                    lo = 64 * odd
                    g = h // R
                    ins = mm(B[7][:, h * 32:h * 32 + NC_], qt[lo:lo + 64, h // 2, t * P:(t + 1) * P],
                             kc[lo:lo + 64, g * NC_:(g + 1) * NC_], start=True, stop=True)
                ins.then_inc(s_cs, 1)
                if odd == 0:
                    pe.wait_ge(s_cs, 2 * t + 1)

        def cmp_transpose(t):
            pe.wait_ge(s_cp, t + 1)
            for g in range(G):
                ins = nc.tensor.transpose(B[7][:, g * P:(g + 1) * P],
                                          pc[:, g * R:(g + 1) * R, :].rearrange("p h n -> p (h n)"), ident[:])
            ins.then_inc(s_ct, 1)

        def head_scores(n):
            t, h = divmod(n, HB)
            lk = P * (t + 1)
            lo = 64 * (h % 2)
            if n >= 3:
                pe.wait_ge(s_ab, n - 2)
            mm(B[n % 3][:, 0:2 * lk], qt[lo:lo + 64, h // 2, t * P:(t + 1) * P], kt[lo:lo + 64, :, h // R, 0:lk],
               start=True, stop=True).then_inc(s_as, 1)

        def head_transpose(n):
            blocks = 2 * (n // HB + 1)
            pe.wait_ge(s_sc, 2 * n + 2)
            if n >= 2:
                pe.wait_ge(s_atc, n - 1)
            for b in range(blocks):
                ins = nc.tensor.transpose(B[(3, 6)[n % 2]][:, b * P:(b + 1) * P], sc[:, n % 3, b * P:(b + 1) * P], ident[:])
            ins.then_inc(s_at, 1)

        def group_out(grp):
            t, g = divmod(grp, G)
            pe.wait_ge(s_atc, R * (grp + 1))
            if g == 0:
                pe.wait_ge(s_ctc, t + 1)
            if grp >= 2:
                pe.wait_ge(s_aol, 2 * (grp - 1))
            bank = B[4 + grp % 2]
            for b in range(2):
                for k in range(t + 1):
                    mm(bank[0:64, :], vv[:, k, b, g * DB:(g + 1) * DB], ptg[grp % 2][:, b * (t + 1) + k, :, :]
                       .rearrange("p r q -> p (r q)"), start=b == 0 and k == 0, stop=False)
            for r in range(R):
                ins = mm(bank[0:64, r * P:(r + 1) * P], vbd[:, g, r * DB:(r + 1) * DB], pct[:, g * P:(g + 1) * P],
                         start=False, stop=r == R - 1)
            ins.then_inc(s_av, 1)

        pe.wait_ge(s_qc, 4)
        pe.wait_ge(s_ngb, 1)
        head_scores(0)
        head_scores(1)
        for n in range(2 * HB):
            t, h = divmod(n, HB)
            if h == 0:
                cmp_scores(t)
            if n + 2 < 2 * HB:
                head_scores(n + 2)
            head_transpose(n)
            if h == 2:
                cmp_transpose(t)
            if n >= R and n % R == 1:
                group_out(n // R - 1)
        group_out(2 * G - 1)
        pe.wait_ge(s_aol, 4 * G)
        for k in range(4):
            down(BO0 + k, (4, 5, 6, 7), 2 * k, k == 0, k == 3)
        transposed(5, 10)
        pe.wait_ge(s_htl, 42)
        small_tokens(B[0], slice(56, 64), 8, 5).then_inc(s_lg, 1)
        pe.wait_ge(s_selm, 1)
        c0, c1 = rt[:, 5, 0:NE], rt[:, 5, NE:2 * NE]
        mm(B[1][:, 0:NE], tri1[:], c0, start=True, stop=True)
        mm(B[1][:, NE:2 * NE], ones[:], c0, start=True, stop=False)
        mm(B[1][:, NE:2 * NE], tri1[:], c1, start=False, stop=True)
        mm(B[1][:, 2 * NE:3 * NE], ones[:], c0, start=True, stop=False)
        mm(B[1][:, 2 * NE:3 * NE], ones[:], c1, start=False, stop=True).then_inc(s_rank, 1)

        def gather(sel_count, job):
            pe.wait_ge(s_sel, sel_count)
            for h in range(2):
                for k in range(4):
                    for t in range(NT):
                        for part in (hg_hi, hg_lo):
                            first, last = t == 0 and part is hg_hi, t == 1 and part is hg_lo
                            ins = mm(B[4 + h][:, k * P:(k + 1) * P], part[:, t, (4 * h + k) * P:(4 * h + k + 1) * P],
                                     sel_oh[:, t, :], start=first, stop=last)
                ins.then_inc(s_ga, 1)
            for t in range(NT):
                mm(B[6][:, 2 * P:2 * P + 1], sel_oh[:, t, :].bitcast(F32), gatej[:, t, job], start=t == 0, stop=t == 1)
            for t in range(NT):
                ins = nc.tensor.transpose(B[6][:, t * P:(t + 1) * P], sel_oh[:, t, :].bitcast(F32), ident[:])
            ins.then_inc(s_gs, 1)

        pe.wait_ge(s_hgl, 2)
        gather(2, slice(0, 1))
        pe.wait_ge(s_tab, 1)
        jobs = pe.value_load(tab[0:1, 0:1], min_val=NE, max_val=NJ_MAX)
        with pe.Fori(0, jobs) as i:
            def gu(s, bank):
                for half in range(2):
                    n = N0 + s + half
                    wait_slot(n, i)
                    for k in range(4):
                        kk = 4 * half + k
                        hi = ht_hi[:, kk // 2, (kk % 2) * P:(kk % 2) * P + P]
                        lo = ht_lo[:, kk // 2, (kk % 2) * P:(kk % 2) * P + P]
                        ins = mm3(bank[:, :], hi, lo, weights(w_hi, n, 512)[:, k, :], weights(w_lo, n, 512)[:, k, :],
                                  kk == 0, kk == 7)
                    ins.then_inc(s_used, 1)

            def job_t(c):
                pe.wait_ge(s_mul, i * 7 + 12 + c + 1)
                if c >= 2:
                    pe.wait_ge(s_tpl, i * 7 + 11 + c - 1)
                for j in range(4):
                    ins = nc.tensor.transpose(B[4 + c % 2][:, j * P:(j + 1) * P], av[:, 0, j * P:(j + 1) * P], ident[:])
                ins.then_inc(s_tp, 1)

            pe.wait_ge(s_gal, i * 2 + 2)
            for c in range(7):
                pe.wait_ge(s_silu, i * 7 + 12 + c)
                if c == 0:
                    pe.wait_ge(s_xu, i * 4 + 12)
                gu(4 * c, B[0])
                if c:
                    job_t(c - 1)
                pe.wait_ge(s_mul, i * 7 + 12 + c)
                gu(4 * c + 2, B[1])
            for d in range(14):
                if d == 1:
                    job_t(6)
                if d == 3:
                    pe.wait_ge(s_tpl, i * 7 + 11 + 7)
                    pe.wait_ge(s_sgc, i + 1)
                    gather(i * 2 + 4, bass.ds(i + 1, 1))
                n = N0 + 28 + d
                wait_slot(n, i)
                if d < 12:
                    pe.wait_ge(s_tpl, i * 7 + 11 + d // 2 + 1)
                for half in range(2):
                    for k in range(2):
                        kk = 2 * d + k
                        w = slice(half * 512, half * 512 + 512)
                        ins = mm3(B[2 + half][:, :], at_hi[:, kk * P:(kk + 1) * P], at_lo[:, kk * P:(kk + 1) * P],
                                  weights(w_hi, n, 1024)[:, k, w], weights(w_lo, n, 1024)[:, k, w],
                                  d == 0 and k == 0, d == 13 and k == 1)
                    if d == 13 and half == 0:
                        ins.then_inc(s_y, 1)
                ins.then_inc(s_used, 1)
            pe.wait_ge(s_gal, i * 2 + 4)
            for n, b in enumerate((0, 1, 7, 5)):
                t, half = divmod(n, 2)
                pe.wait_ge(s_yc, i * 2 + half + 1)
                mm(B[b][:, :], selt[:, t * P:(t + 1) * P], ysb[:, half * 512:(half + 1) * 512], start=True,
                   stop=True).then_inc(s_scat, 1)

    ctx.close()


def kernel(**inputs):
    import numpy as np
    from concourse import bacc
    from concourse.bass_utils import run_bass_kernel_spmd

    f = {k: np.asarray(v) for k, v in inputs.items()}

    def columns(v):
        return v.reshape(KD, P).T

    gains = [f["norm_mix"][0], f["a_norm_h"][0], f["norm_ffn"][0], f["norm_kv"], f["norm_mix"][1],
             np.ones(D, np.float32), f["norm_ffn"][1]]
    packed = np.zeros((P, C_END), np.float32)
    for n, g in enumerate(gains):
        packed[:, C_GAIN + 8 * n:C_GAIN + 8 * n + 8] = columns(g)
    packed[:, C_CONV:C_CONV + 64] = f["a_conv"][0].reshape(4, 16, P).transpose(2, 1, 0).reshape(P, 64)
    packed[0:4, C_BIF] = f["a_b_gate"][0, 0:4]
    packed[0:4, C_BIF + 1] = f["a_b_gate"][0, 4:8]
    packed[:, C_BG:C_BG + 48] = f["b_b_gate"][0][None, :]
    packed[:, C_POS:C_POS + 32] = f["b_cmp_pos"].reshape(16, 2, 2, DB).transpose(1, 3, 2, 0).reshape(P, 32)
    packed[:, C_W2:C_W2 + 256] = f["b_cmp_w2"].reshape(2, 2, P, DB).transpose(2, 0, 1, 3).reshape(P, 256)
    ws = np.concatenate([f["a_w_in"][0][:, 4 * D:], f["b_w_q"][0][:, D:], f["m_router"][0]], axis=1)
    packed[:, C_WS:C_WS + 512] = ws.reshape(KD, P, 64).transpose(1, 0, 2).reshape(P, 512)

    arrays = {"x": f["x"], "packed": packed, "a_w_in": f["a_w_in"], "a_w_out": f["a_w_out"], "b_w_kv": f["b_w_kv"],
              "b_cmp_w1": f["b_cmp_w1"], "b_w_q": f["b_w_q"], "b_w_out": f["b_w_out"], "f_w_gu": f["f_w_gu"],
              "f_w_down": f["f_w_down"], "m_w_gu": f["m_w_gu"], "m_w_down": f["m_w_down"],
              "norm_ffn1": f["norm_ffn"][1:2], "norm_final": f["norm_final"][None, :]}
    arrays = {k: np.ascontiguousarray(v) for k, v in arrays.items()}
    nc = bacc.Bacc("TRN2", target_bir_lowering=False, num_devices=1)
    aps = [nc.dram_tensor(f"in_{k}", v.shape, mybir.dt.float32, kind="ExternalInput").ap() for k, v in arrays.items()]
    out = nc.dram_tensor("out", (1, T, D), mybir.dt.float32, kind="ExternalOutput").ap()
    trunk(nc, *aps, out)
    r = run_bass_kernel_spmd(nc, [{f"in_{k}": v for k, v in arrays.items()}], core_ids=[0])
    return r.results[0]["out"]
```

```python
import concourse.bass as bass
from concourse import mybir
from contextlib import ExitStack

P = 128
D, T = 1024, 256
NT, KD = T // P, D // P
HA, DA = 4, 256
HB, DB, G, R = 16, 64, 4, 4
NC_, CL, CS = 15, 32, 16
CH = 256
FD, NE, FE = 2816, 8, 3584
EPS = 1e-6
NEG = -1e30
SLOT = 2048
RAW, SPLIT = 7, 3
NJ_MAX = 11
JOB_SLOTS = 7 * 4 + 14
XW = 2 * 16 * G * NC_ + 12
XM = G * NC_ + 12
AHEAD = 2
SC = 4
TURN = 3

C_GAIN = 0
C_CONV = C_GAIN + 56
C_BIF = C_CONV + 64
C_BG = C_BIF + 2
C_POS = C_BG + 48
C_W2 = C_POS + 32
C_WS = C_W2 + 256
WS = 72
C_END = C_WS + KD * WS


def trunk(nc, x, packed, a_w_in, a_w_out, b_w_kv, b_cmp_w1, b_w_q, b_w_out, f_w_gu, f_w_down,
          m_w_gu, m_w_down, norm_ffn1, norm_final, out):
    F32, FR, I32 = mybir.dt.float32, mybir.dt.float32r, mybir.dt.int32
    ALU, ACT, AX = mybir.AluOpType, mybir.ActivationFunctionType, mybir.AxisListType
    ctx = ExitStack()
    ctx.enter_context(nc.allow_non_contiguous_dma("weights"))

    edge = [(nc.sbuf_base + 31) // 32 * 32]

    def sb(name, shape, dt=F32, at=None):
        size = 4
        for n in shape[1:]:
            size *= n
        if at is None:
            at = edge[0]
            edge[0] = (at + size + 31) // 32 * 32
        return nc.alloc_sbuf_tensor_at(name, list(shape), dt, offset=at), at

    raw, _ = sb("raw", [P, RAW, SLOT])
    w_hi, _ = sb("w_hi", [P, SPLIT, SLOT], FR)
    w_lo, _ = sb("w_lo", [P, SPLIT, SLOT], FR)
    xs, _ = sb("xs", [P, NT, D])
    xn, xn_at = sb("xn", [P, NT, D])
    ht_hi, ht_at = sb("ht_hi", [P, KD, T], FR)
    ht_lo, _ = sb("ht_lo", [P, KD, T], FR)
    at_hi, a0 = sb("at_hi", [P, 22 * T], FR)
    at_lo, _ = sb("at_lo", [P, 22 * T], FR)
    arena_end = edge[0]
    sg, sg_at = sb("sg", [P, NT, 512])
    av, _ = sb("av", [P, NT, 512])
    pk, _ = sb("pk", [P, C_END])
    ws_hi, _ = sb("ws_hi", [P, KD, WS], FR)
    ws_lo, _ = sb("ws_lo", [P, KD, WS], FR)
    ident, _ = sb("ident", [P, P])
    tri_mask, _ = sb("tri_mask", [P, T])
    small, small_at = sb("small", [P, 512])
    sel_oh, _ = sb("sel_oh", [P, NT, P], FR)
    slot_iota, _ = sb("slot_iota", [P, P])
    rows, _ = sb("rows", [4, 8, T], F32, sg_at)

    o = a0
    qk, _ = sb("qk", [P, 16, T], F32, o); o += 16 * T * 4
    va, _ = sb("va", [P, NT, HA, DA + 1], F32, o); o += NT * HA * (DA + 1) * 4
    og, _ = sb("og", [P, NT, D], F32, o); o += NT * D * 4
    wd, _ = sb("wd", [P, HA, 384], F32, o); o += HA * 384 * 4
    pd, _ = sb("pd", [P, 2, 384], F32, o); o += 2 * 384 * 4
    nsel, _ = sb("nsel", [4, HA, P], F32, o); o += HA * P * 4
    assert o <= arena_end
    o = a0
    kt, _ = sb("kt", [P, 2, G, T], F32, o); o += 2 * G * T * 4
    vv, _ = sb("vv", [P, NT, 2, G * DB], F32, o); o += NT * 2 * G * DB * 4
    qt, _ = sb("qt", [P, 8, T], F32, o); o += 8 * T * 4
    ct_at = o
    ct, _ = sb("ct", [P, 2, G, T], F32, o); o += 2 * G * T * 4
    xf_at = o
    xf, _ = sb("xf", [P, XW], F32, o); o += (XW * 4 + 31) // 32 * 32
    hidt, _ = sb("hidt", [P, 2, 2, G * NC_], F32, o); o += 4 * G * NC_ * 4
    vbd, _ = sb("vbd", [P, G, R * DB], F32, o); o += G * R * DB * 4
    kc, _ = sb("kc", [P, G * NC_], F32, o); o += 64 * 4
    dat, _ = sb("dat", [P, NT, T], F32, o); o += NT * T * 4
    att, _ = sb("att", [P, 2, 2, 32], F32, o); o += 128 * 4
    gat, _ = sb("gat", [P, NT, 48], F32, o); o += 96 * 4
    coef, _ = sb("coef", [P, 2, 32], F32, o); o += 64 * 4
    assert o <= arena_end, (o, arena_end)
    xc_hi, _ = sb("xc_hi", [P, XW], FR, ct_at)
    xc_lo, _ = sb("xc_lo", [P, XW], FR, sg_at)
    hid, _ = sb("hid", [G * NC_, 2, CH], F32, small_at)
    sc, _ = sb("sc", [P, SC, 512], F32, xf_at)
    ptg = [sb("pt_even", [P, 4, R, P], F32, sg_at)[0], sb("pt_odd", [P, 4, R, P], F32, ct_at)[0]]
    pc, _ = sb("pc", [P, HB, 32], F32, small_at)
    hg_hi, _ = sb("hg_hi", [P, NT, D], FR, a0 + 28 * P * 4)
    hg_lo, _ = sb("hg_lo", [P, NT, D], FR, a0 + 22 * T * 4 + 28 * P * 4)
    pct, _ = sb("pct", [P, NT, 512], F32, xn_at)
    rows_g, _ = sb("rows_g", [P, D], F32, xn_at)
    y_hi, _ = sb("y_hi", [P, D], FR, xn_at)
    y_lo, _ = sb("y_lo", [P, D], FR, xn_at + D * 4)
    g1b, _ = sb("g1b", [P, D], F32, sg_at)
    gfb, _ = sb("gfb", [P, D], F32, ht_at)
    dcb, dcb_at = sb("dcb", [P, NT, HB, NC_])
    cval, _ = sb("cval", [P, NT, NC_])
    ones, _ = sb("ones", [P, P])
    tri1, _ = sb("tri1", [P, P])
    tri8, _ = sb("tri8", [P, NE, NE])
    selt, _ = sb("selt", [P, 2 * P], FR)
    gcol, _ = sb("gcol", [P, 1])
    iot, _ = sb("iot", [P, NE])
    tab, _ = sb("tab", [1, 16], I32)
    posj, _ = sb("posj", [P, NT, 12])
    gatej, _ = sb("gatej", [P, NT, 12])
    consts, _ = sb("consts", [P, 4])
    stats, _ = sb("stats", [P, 64])
    cmx, _ = sb("cmx", [P, 2, HB])
    big8, _ = sb("big8", [P, 2, NT * NE * NE], F32, dcb_at)
    rt, _ = sb("rt", [P, 16, NT * NE])
    assert edge[0] <= nc.sbuf_usable_end, edge[0]

    B = [ctx.enter_context(nc.psum_tensor(f"bank{i}", [P, 512], F32)) for i in range(8)]

    def sem(name):
        return ctx.enter_context(nc.semaphore(name))

    landed = [sem(f"landed{i}") for i in range(RAW)]
    s_hi, s_lo, s_used, s_hh = sem("hi_ready"), sem("lo_ready"), sem("slot_used"), sem("half_hi_ready")
    s_x = [sem(f"x_landed{t}") for t in range(NT)]
    s_pk, s_g1b, s_gfb = sem("packed_landed"), sem("ffn_gain_landed"), sem("final_gain_landed")
    s_out = sem("out_stored")
    s_pc = sem("pool_chain"); s_ac = sem("act_chain"); s_dc = sem("dve_chain")
    s_const = sem("constants_ready")
    s_wshi, s_wslo = sem("small_hi"), sem("small_lo")
    s_sq, s_rstd, s_xn = sem("squares_summed"), sem("rstd_ready"), sem("xn_ready")
    s_xt, s_hth, s_htl = sem("transposed"), sem("ht_hi_ready"), sem("ht_lo_ready")
    s_y, s_xu = sem("y_ready"), sem("x_updated")
    s_gp, s_rows = sem("gate_product"), sem("rows_ready")
    s_sf, s_sfc = sem("small_features"), sem("small_features_copied")
    s_lnx, s_lnd = sem("softplus_in"), sem("softplus_out")
    s_cols, s_colc, s_nm = sem("gate_columns"), sem("columns_copied"), sem("max_rows")
    s_arg, s_wd = sem("arg_ready"), sem("decay_ready")
    s_qka, s_conv = sem("tap_applied"), sem("conv_done")
    s_v, s_vc, s_o, s_oc = sem("v_product"), sem("v_copied"), sem("o_product"), sem("o_gated")
    s_s, s_p, s_num, s_den, s_hs = sem("scores"), sem("weighted"), sem("numerator"), sem("inv_den"), sem("h_scaled")
    s_hq, s_hr = sem("h_squares"), sem("h_rstd")
    s_g, s_silu, s_u, s_mul = sem("gate_half"), sem("silu_done"), sem("up_half"), sem("act_done")
    s_tp, s_tph, s_tpl = sem("act_transposed"), sem("at_hi_ready"), sem("at_lo_ready")
    s_kva, s_kvd = sem("kv_copied_act"), sem("kv_copied_dve")
    s_xf, s_xch = sem("blocks_ready"), sem("blocks_hi")
    s_hid, s_hidt, s_hidc = sem("hidden_ready"), sem("hidden_transposed"), sem("hidden_t_copied")
    s_w2, s_kc = sem("compressed"), sem("compressed_copied")
    s_qc = sem("q_copied")
    s_ng, s_ngb, s_nge = sem("nsa_gates"), sem("nsa_gates_biased"), sem("nsa_gates_exp")
    s_cs, s_cb, s_ce, s_cp = sem("cmp_scores"), sem("cmp_biased"), sem("cmp_exp"), sem("cmp_probs")
    s_ct, s_ctc = sem("cmp_transposed"), sem("cmp_t_copied")
    s_as, s_ab, s_ae = sem("att_scores"), sem("att_biased"), sem("att_exp")
    s_cf, s_sca, s_scd = sem("coefficients_ready"), sem("att_scaled_act"), sem("att_scaled_dve")
    s_at, s_atc, s_av = sem("att_transposed"), sem("att_t_copied"), sem("att_out")
    s_aoh, s_aol = sem("att_out_hi"), sem("att_out_lo")
    s_hgx, s_hgh, s_hgl = sem("gained"), sem("gained_hi"), sem("gained_lo")
    s_lg, s_le, s_lex = sem("logits"), sem("logits_shifted"), sem("logits_exp")
    s_selm, s_rank, s_tab = sem("chosen"), sem("ranked"), sem("jobs_ready")
    s_sel, s_gs, s_sgc = sem("one_hot"), sem("places"), sem("places_copied")
    s_ga, s_gr, s_gt = sem("gathered"), sem("gathered_copied"), sem("gathered_transposed")
    s_gah, s_gal = sem("gathered_hi"), sem("gathered_lo")
    s_gc, s_gates = sem("place_gates_copied"), sem("token_gates_ready")
    s_yh, s_yl, s_scat, s_fin = sem("y_hi_ready"), sem("y_lo_ready"), sem("scattered"), sem("final_ready")

    def kp(w):
        return w.rearrange("(k p) n -> p k n", p=P)

    w_in, w_o, w_kv, w_q, w_bo = kp(a_w_in[0]), kp(a_w_out[0]), kp(b_w_kv), kp(b_w_q[0]), kp(b_w_out[0])
    w_gu, w_dn = kp(f_w_gu[0]), kp(f_w_down[0])
    slots = []
    QK0 = 0
    slots += [w_in[:, :, c * 256:(c + 1) * 256] for c in range(8)]
    V0 = len(slots)
    for c in range(4):
        slots += [w_in[:, k:k + 4, 2 * D + c * 512:2 * D + (c + 1) * 512] for k in (0, 4)]
    O0 = V0 + 4
    WO0 = len(slots)
    slots += [w_o[:, 2 * k:2 * k + 2, :] for k in range(4)]
    FF0 = len(slots)
    for c in range(5):
        for base in (0, FD):
            slots += [w_gu[:, k:k + 4, base + c * 512:base + (c + 1) * 512] for k in (0, 4)]
    slots += [w_gu[:, :, base + 2560:base + 2816] for base in (0, FD)]
    DN0 = len(slots)
    slots += [w_dn[:, 2 * k:2 * k + 2, :] for k in range(11)]
    KV0 = len(slots)
    KV_ORDER = (0, 1, 2, 4, 3, 5)
    slots += [w_kv[:, :, b * 256:(b + 1) * 256] for b in KV_ORDER]
    W10 = len(slots)
    for c in range(2):
        slots += [kp(b_cmp_w1[c])[:, j:j + 8, :] for j in (0, 8)]
    Q0 = len(slots)
    slots += [w_q[:, :, c * 256:(c + 1) * 256] for c in range(4)]
    BO0 = len(slots)
    slots += [w_bo[:, 2 * k:2 * k + 2, :] for k in range(4)]
    N0 = len(slots)

    e_gu = m_w_gu.rearrange("l e (k p) n -> (l e) p k n", p=P)
    e_dn = m_w_down.rearrange("l e (k p) n -> (l e) p k n", p=P)

    def job_slot(e, s):
        if s < 28:
            c, part = divmod(s, 4)
            col = (part // 2) * FE + c * 512
            k0 = (part % 2) * 4
            v = e_gu[e, :, k0:k0 + 4, col:col + 512]
        else:
            k0 = 2 * (s - 28)
            v = e_dn[e, :, k0:k0 + 2, :]
        return v.rearrange("e p k n -> p (e k) n")

    def weights(buf, n, b):
        ring = {id(raw): RAW}.get(id(buf), SPLIT)
        return buf[:, n % ring, :].rearrange("p (a b) -> p a b", b=b)

    def num_banks(h):
        return (B[4], B[5]) if h == HA - 1 else (B[6], B[7])

    def tile_ready(engine, sem_, c, t, n):
        if t == 0:
            engine.wait_ge(sem_, c + 1)
        else:
            engine.wait_ge(s_used, n + 1)

    block = ctx.enter_context(nc.Block())

    @block.sync
    def _(sp):
        def load(n, src, base=0, off=0):
            if base or n >= RAW:
                sp.wait_ge(s_lo, off + n - RAW + 1)
            sp.dma_start(weights(raw, n, src.shape[2]), src).then_inc(landed[n % RAW], 16)

        sp.dma_start(xs[:, 0, :], x[0, 0:P, :]).then_inc(s_x[0], 16)
        sp.dma_start(xs[:, 1, :], x[0, P:T, :]).then_inc(s_x[1], 16)
        sp.dma_start(pk[:], packed).then_inc(s_pk, 16)
        for n in range(N0):
            load(n, slots[n])
        with sp.Fori(0, NE) as i:
            for s in range(JOB_SLOTS):
                load(N0 + s, job_slot(bass.ds(i, 1), s), 1, i * JOB_SLOTS)
        sp.wait_ge(s_tab, 1)
        jobs = sp.value_load(tab[0:1, 0:1], min_val=NE, max_val=NJ_MAX)
        with sp.If(jobs > NE):
            with sp.Fori(NE, jobs) as i:
                e = sp.value_load(tab[0:1, bass.ds(i - (NE - 1), 1)], min_val=0, max_val=NE - 1)
                for s in range(JOB_SLOTS):
                    load(N0 + s, job_slot(bass.ds(e, 1), s), 1, i * JOB_SLOTS)
        for s in range(TURN):
            load(N0 + s, job_slot(slice(0, 1), s), 1, jobs * JOB_SLOTS)
        sp.wait_ge(s_used, jobs * JOB_SLOTS + N0 + 1)
        sp.dma_start(gfb[:], norm_final.partition_broadcast(P).rearrange("p a d -> p (a d)")).then_inc(s_gfb, 16)
        for t in range(NT):
            sp.wait_ge(s_fin, t + 1)
            sp.dma_start(out[0, t * P:(t + 1) * P, :], xn[:, t, :]).then_inc(s_out, 16)
        sp.wait_ge(s_out, 16 * NT)

    @block.gpsimd
    def _(pool):
        n = [0]
        g = nc.gpsimd

        def step(ins):
            n[0] += 1
            ins.then_inc(s_pc, 1)
            pool.wait_ge(s_pc, n[0])

        step(g.memset(ident[:], 0.0))
        step(g.affine_select(out=ident[:], in_=ident[:], compare_op=ALU.not_equal, fill=1.0, base=0,
                             pattern=[[-1, P]], channel_multiplier=1))
        step(g.memset(consts[:, 0:1], -0.5))
        step(g.memset(consts[:, 1:2], 1.0))
        step(g.memset(consts[:, 2:3], 0.0))
        step(g.memset(ones[:], 1.0))
        step(g.memset(nsel[:], 0.0))
        step(g.affine_select(out=nsel[:], in_=nsel[:], compare_op=ALU.not_equal, fill=-1.0, base=0,
                             pattern=[[-1, HA], [0, P]], channel_multiplier=1))
        step(g.memset(tri_mask[:], 0.0))
        step(g.affine_select(out=tri_mask[:, 0:P], in_=tri_mask[:, 0:P], compare_op=ALU.is_ge, fill=NEG,
                             base=0, pattern=[[1, P]], channel_multiplier=-1))
        g.memset(va[:, :, :, DA:DA + 1], 1.0).then_inc(s_const, 1)

        rr = [0]

        def rstd(m, scale, dst, src):
            pool.wait_ge(m[0], m[1])
            step(g.tensor_scalar(dst, src, scale, EPS, ALU.mult, ALU.add))
            w = dst.shape[1]
            rr[0] += 1
            return g.tensor_tensor(dst, dst, consts[:, 0:1].broadcast_to([P, w]), ALU.pow)

        def norm_rstd(i):
            for t in range(NT):
                rstd((s_sq, NT * i + t + 1), 1.0 / D, stats[:, 2 + 4 * i + t:3 + 4 * i + t],
                     stats[:, 4 * i + t:4 * i + t + 1]).then_inc(s_rstd, 1)

        norm_rstd(0)
        for t in range(NT):
            step(g.iota(cval[:, t, :], [[CS, NC_]], base=CL - 1 - t * P, channel_multiplier=-1,
                        allow_small_or_imprecise_dtypes=True))
            step(g.affine_select(out=cval[:, t, :], in_=cval[:, t, :], compare_op=ALU.is_ge, fill=NEG,
                                 base=t * P - (CL - 1), pattern=[[-CS, NC_]], channel_multiplier=1))
            for h in range(HB):
                step(g.tensor_scalar(dcb[:, t, h, :], cval[:, t, :], float(2.0 ** (-8.0 * (h + 1) / HB)), None, ALU.mult))
            step(g.memset(cval[:, t, :], 1.0))
            step(g.affine_select(out=cval[:, t, :], in_=cval[:, t, :], compare_op=ALU.is_ge, fill=0.0,
                                 base=t * P - (CL - 1), pattern=[[-CS, NC_]], channel_multiplier=1))
        step(g.memset(tri1[:], 1.0))
        step(g.affine_select(out=tri1[:], in_=tri1[:], compare_op=ALU.is_gt, fill=0.0, base=0,
                             pattern=[[1, P]], channel_multiplier=-1))
        step(g.memset(tri8[:], 1.0))
        step(g.affine_select(out=tri8[:], in_=tri8[:], compare_op=ALU.is_gt, fill=0.0, base=0,
                             pattern=[[1, NE], [-1, NE]], channel_multiplier=0))
        step(g.iota(slot_iota[:], [[1, P]], base=0, channel_multiplier=0, allow_small_or_imprecise_dtypes=True))
        g.iota(iot[:], [[1, NE]], base=0, channel_multiplier=0, allow_small_or_imprecise_dtypes=True).then_inc(s_const, 1)
        for b in range(2):
            rstd((s_hq, 4 * (b + 1)), 1.0 / DA, stats[:, 44 + 4 * b:48 + 4 * b], stats[:, 36 + 4 * b:40 + 4 * b]).then_inc(s_hr, 1)
        norm_rstd(1)
        norm_rstd(2)
        pool.wait_ge(s_xu, 8)
        for t in range(NT):
            step(g.iota(dat[:, t, :], [[1, T]], base=-t * P, channel_multiplier=-1, allow_small_or_imprecise_dtypes=True))
            step(g.affine_select(out=dat[:, t, :], in_=dat[:, t, :], compare_op=ALU.is_ge, fill=NEG,
                                 base=t * P, pattern=[[-1, T]], channel_multiplier=1))
        step(g.memset(xf[:, XW - 12:XW], 0.0))
        g.memset(vbd[:], 0.0).then_inc(s_const, 1)
        pool.wait_ge(s_hidt, 1)
        g.memset(pc[:], 0.0).then_inc(s_const, 1)
        norm_rstd(3)
        norm_rstd(4)

    @block.scalar
    def _(act):
        a = nc.scalar.activation
        done = [0]

        def split_to(m):
            while done[0] <= min(m, N0 - 1 + TURN):
                n = done[0]
                act.wait_ge(landed[n % RAW], 16 * (n // RAW + 1))
                if n >= SPLIT:
                    act.wait_ge(s_used, n - SPLIT + 1)
                a(w_hi[:, n % SPLIT, :], raw[:, n % RAW, :], ACT.Copy).then_inc(s_hi, 1)
                done[0] += 1

        def split_half(n, second):
            if not second:
                act.wait_ge(landed[n % RAW], 16 * (n // RAW + 1))
                act.wait_ge(s_used, n - SPLIT + 1)
            w = slice(1024 * second, 1024 * second + 1024)
            a(w_hi[:, n % SPLIT, w], raw[:, n % RAW, w], ACT.Copy).then_inc(s_hi if second else s_hh, 1)
            if second:
                done[0] += 1

        def squares(i, updates=None):
            for t in range(NT):
                if updates is not None:
                    act.wait_ge(s_xu, updates + 2 * (t + 1))
                else:
                    act.wait_ge(s_x[t], 16)
                a(xn[:, t, :], xs[:, t, :], ACT.Square, accum_out=stats[:, 4 * i + t:4 * i + t + 1]).then_inc(s_sq, 1)

        def ht_high(p, gain, banks=(0, 1, 2, 3)):
            for b in range(4):
                act.wait_ge(s_xt, 4 * p + b + 1)
                for k in (2 * b, 2 * b + 1):
                    a(ht_hi[:, k, :], B[banks[b]][:, (k % 2) * 256:(k % 2) * 256 + 256], ACT.Copy,
                      scale=pk[:, C_GAIN + 8 * gain + k:C_GAIN + 8 * gain + k + 1]).then_inc(s_hth, 1)

        squares(0)
        act.wait_ge(s_pk, 16)
        a(ws_hi[:].rearrange("p k n -> p (k n)"), pk[:, C_WS:C_END], ACT.Copy).then_inc(s_wshi, 1)
        ht_high(0, 0)
        split_to(0)

        def softplus():
            act.wait_ge(s_lnx, 1)
            a(rows[:, 2, :], rows[:, 2, :], ACT.Exp, scale=-1.0).then_inc(s_ac, 1)
            act.wait_ge(s_ac, 1)
            a(rows[:, 2, :], rows[:, 2, :], ACT.Ln, bias=consts[0:4, 1:2]).then_inc(s_lnd, 1)

        def em_rows():
            act.wait_ge(s_rows, 1)
            a(rows[:, 7, :], rows[:, 6, :], ACT.Exp, scale=-1.0).then_inc(s_rows, 1)
            act.wait_ge(s_cols, 1)
            a(small[:, 16:32], B[5][:, 0:16], ACT.Copy).then_inc(s_colc, 1)

        for s in range(8):
            split_to(s + AHEAD)
            act.wait_ge(s_used, QK0 + s + 1)
            for b in (0, 1):
                blk = 2 * s + b
                a(qk[:, blk, :], B[s % 3][:, b * 256:b * 256 + 256], ACT.Copy,
                  scale=pk[:, C_CONV + 4 * blk + 3:C_CONV + 4 * blk + 4]).then_inc(s_qka, 1)
            if s == 1:
                softplus()
            if s == 3:
                em_rows()
        split_to(V0 + AHEAD)
        for h in range(HA):
            act.wait_ge(s_arg, 2 * h + 2)
            act.wait_ge(s_colc, 1)
            a(wd[:, h, 0:T], wd[:, h, 0:T], ACT.Exp, bias=small[:, 16 + h:17 + h]).then_inc(s_wd, 1)
            a(wd[:, h, T:384], wd[:, h, T:384], ACT.Exp, bias=small[:, 20 + h:21 + h]).then_inc(s_wd, 1)
        for c in range(2):
            split_to(V0 + 2 * c + 1 + AHEAD)
            for t in range(NT):
                tile_ready(act, s_v, c, t, V0 + 2 * c + 1)
                a(va[:, t, 2 * c:2 * c + 2, 0:DA], B[2 + t - 2 * c][:, :].rearrange("p (h d) -> p h d", h=2),
                  ACT.Copy).then_inc(s_vc, 1)

        def o_gate(c):
            for t in range(NT):
                tile_ready(act, s_o, c, t, O0 + 2 * c + 1)
                a(og[:, t, c * 512:(c + 1) * 512], B[2 + t - 2 * c][:, :], ACT.Sigmoid).then_inc(s_oc, 1)

        def head_out(h):
            act.wait_ge(s_den, h + 1)
            for t in range(NT):
                a(xn[:, t, h * DA:(h + 1) * DA], num_banks(h)[t][:, 0:DA], ACT.Copy,
                  scale=stats[:, 52 + t:53 + t]).then_inc(s_hs, 1)
            for t in range(NT):
                act.wait_ge(s_hs, 2 * h + t + 1)
                col = 36 + 4 * (h // 2) + 2 * (h % 2) + t
                a(wd[:, h, 0:DA], xn[:, t, h * DA:(h + 1) * DA], ACT.Square,
                  accum_out=stats[:, col:col + 1]).then_inc(s_hq, 1)
                act.wait_ge(s_hq, 2 * h + t + 1)

        for h in range(HA):
            split_to(O0 + h + AHEAD)
            if h == 3:
                head_out(3)
            if h == 2:
                o_gate(0)
            if h < 3:
                head_out(h)
        split_to(WO0 + AHEAD - 1)
        o_gate(1)
        ht_high(1, 1)
        split_to(FF0 - 1 + AHEAD)
        squares(1, 0)
        ht_high(2, 2)

        def act_high(bank, dst, n):
            act.wait_ge(s_tp, n)
            a(dst, bank, ACT.Copy).then_inc(s_tph, 1)

        def dense_high(c):
            for b in range(2 if c < 5 else 1):
                act_high(B[4 + b][:, :], at_hi[:, (4 * c + 2 * b) * T:(4 * c + 2 * b + 2) * T], 2 * c + b + 1)

        for c in range(6):
            n = FF0 + 4 * c
            width = 512 if c < 5 else 256
            split_to(n + (1 if c < 5 else 0) + AHEAD)
            for t in range(NT):
                tile_ready(act, s_g, c, t, n + (1 if c < 5 else 0))
                if c:
                    act.wait_ge(s_mul, 2 * c)
                a(sg[:, t, 0:width], B[t][:, 0:width], ACT.Silu).then_inc(s_silu, 1)
            if c:
                dense_high(c - 1)
            split_to(n + (3 if c < 5 else 1) + AHEAD)
        dense_high(5)
        split_to(KV0 - 1 + AHEAD)
        squares(2, 4)
        ht_high(3, 3)
        for i in range(6):
            split_to(KV0 + i + AHEAD)
            act.wait_ge(s_used, KV0 + i + 1)
            bank = B[4 + i % 2]
            lower = bank[0:64, :].rearrange("p (b t) -> p b t", b=2)
            if i < 2:
                a(ct[0:64, i, 0::2, :], lower, ACT.Copy).then_inc(s_kva, 1)
                a(ct[64:128, i, 0::2, 0:T - 1], lower[:, :, 1:T], ACT.Copy).then_inc(s_kva, 1)
            elif i < 4:
                a(kt[0:64, i - 2, 0::2, :], lower, ACT.Copy).then_inc(s_kva, 1)
                a(kt[64:128, i - 2, 0::2, :], lower, ACT.Copy).then_inc(s_kva, 1)
            else:
                a(vv[:, :, i - 4, :], bank[:, :].rearrange("p (t d) -> p t d", t=2), ACT.Copy).then_inc(s_kva, 2)
            if i == 3:
                act.wait_ge(s_xf, 2)
                act.wait_ge(s_const, 3)
                a(xc_hi[:], xf[:], ACT.Copy).then_inc(s_xch, 1)
        act.wait_ge(s_used, W10)
        ht_high(4, 4)
        for c in range(2):
            split_to(W10 + 2 * c + 1 + AHEAD)
            act.wait_ge(s_used, W10 + 2 * c + 2)
            a(hid[:, c, :], B[6 + c][0:G * NC_, 0:CH], ACT.Silu).then_inc(s_hid, 1)
        act.wait_ge(s_hidt, 1)
        a(hidt[:].rearrange("p c h n -> p (c h n)"), B[4][:, 0:4 * G * NC_], ACT.Copy).then_inc(s_hidc, 1)
        act.wait_ge(s_w2, 1)
        a(kc[:, 0:G * NC_], B[5][:, 0:G * NC_], ACT.Copy).then_inc(s_kc, 1)
        for r in range(R):
            a(vbd[32 * r:32 * r + NC_, :, r * DB:(r + 1) * DB],
              B[6][0:NC_, 0:G * DB].rearrange("p (g d) -> p g d", g=G), ACT.Copy).then_inc(s_kc, 1)
        for i in range(4):
            split_to(Q0 + i + AHEAD)
            act.wait_ge(s_used, Q0 + i + 1)
            a(qt[:, 2 * i:2 * i + 2, :], B[i % 2][:, :].rearrange("p (b t) -> p b t", b=2), ACT.Copy,
              scale=DB ** -0.5).then_inc(s_qc, 1)
            if i == 1:
                act.wait_ge(s_sf, 1)
                a(sc[0:WS, 2, 0:T], B[2][0:WS, 0:T], ACT.Copy).then_inc(s_sfc, 1)
            if i == 2:
                act.wait_ge(s_ngb, 2)
                a(gat[:].rearrange("p t n -> p (t n)"), gat[:].rearrange("p t n -> p (t n)"), ACT.Exp,
                  scale=-1.0).then_inc(s_nge, 1)

        def cmp_exp(t):
            act.wait_ge(s_cb, t + 1)
            a(pc[:, :, 0:NC_], pc[:, :, 0:NC_], ACT.Exp).then_inc(s_ce, 1)

        def cmp_t(t):
            act.wait_ge(s_ct, t + 1)
            a(pct[:, t, :], B[7][:, :], ACT.Copy).then_inc(s_ctc, 1)

        def head_exp(n):
            lk = P * (n // HB + 1)
            act.wait_ge(s_ab, n + 1)
            for b in range(2):
                v = sc[:, n % SC, b * lk:(b + 1) * lk]
                a(v, v, ACT.Exp, bias=att[:, 0, b, n:n + 1], accum_out=att[:, 1, b, n:n + 1]).then_inc(s_ae, 1)

        def head_t(n):
            blocks = 2 * (n // HB + 1)
            act.wait_ge(s_at, n + 1)
            grp = n // R
            if grp >= 2:
                act.wait_ge(s_av, grp - 1)
            a(ptg[grp % 2][:, 0:blocks, n % R, :], B[(3, 6)[n % 2]][:, 0:blocks * P].rearrange("p (b q) -> p b q", b=blocks),
              ACT.Copy).then_inc(s_atc, 1)

        def group_high(grp):
            t, g = divmod(grp, G)
            act.wait_ge(s_av, grp + 1)
            for odd in range(2):
                a(ht_hi[64 * odd:64 * odd + 64, 2 * g:2 * g + 2, t * P:(t + 1) * P],
                  B[4 + grp % 2][0:64, :].rearrange("p (k o q) -> p o k q", k=2, o=2)[:, odd, :, :],
                  ACT.Copy).then_inc(s_aoh, 1)

        head_exp(0)
        for n in range(2 * HB):
            first = sc[:, n % SC, 0:P * (n // HB + 1)]
            act.wait_ge(s_cf, n + 1)
            a(first, first, ACT.Copy, scale=coef[:, 0, n:n + 1]).then_inc(s_sca, 1)
            if n + 1 < 2 * HB:
                head_exp(n + 1)
            if n in (2, 14):
                cmp_exp(n // 14)
            if n:
                head_t(n - 1)
            if n in (4, 18):
                cmp_t(n // 18)
            if n > 2 * R and n % R == 1:
                group_high(n // R - 2)
            if n in (24, 26):
                split_half(BO0 + 2, n == 26)
        head_t(2 * HB - 1)
        group_high(2 * G - 2)
        split_to(BO0 + 3)
        group_high(2 * G - 1)
        act.dma_start(g1b[:], norm_ffn1.partition_broadcast(P).rearrange("p a d -> p (a d)")).then_inc(s_g1b, 16)
        split_to(N0 - 1 + AHEAD)
        squares(3, 8)
        split_to(N0 - 1 + TURN)
        ht_high(5, 6)
        act.wait_ge(s_sf, 2)
        a(small[0:WS, 0:T], B[4][0:WS, 0:T], ACT.Copy).then_inc(s_sfc, 1)
        for t in range(NT):
            act.wait_ge(s_hgx, t + 1)
            a(hg_hi[:, t, :], xn[:, t, :], ACT.Copy).then_inc(s_hgh, 1)
        act.wait_ge(s_le, 1)
        a(rt[:, 2, :], rt[:, 1, :], ACT.Exp).then_inc(s_lex, 1)

        def gathered_rows(n):
            for h in range(2):
                act.wait_ge(s_ga, n + h + 1)
                a(rows_g[:, h * 512:(h + 1) * 512], B[h][:, :], ACT.Copy).then_inc(s_gr, 1)

        def gathered_high(n):
            for h in range(2):
                act.wait_ge(s_gt, n + h + 1)
                a(ht_hi[:, 2 * h:2 * h + 2, :].rearrange("p k t -> p (k t)"), B[4 + h][:, :], ACT.Copy).then_inc(s_gah, 1)

        gathered_rows(0)
        gathered_high(0)
        act.wait_ge(s_tab, 1)
        jobs = act.value_load(tab[0:1, 0:1], min_val=NE, max_val=NJ_MAX)
        with act.Fori(0, jobs) as i:
            nxt = [TURN]

            def split(m):
                while nxt[0] <= m:
                    n = N0 + nxt[0]
                    act.wait_ge(landed[n % RAW], i * (16 * JOB_SLOTS // RAW) + 16 * (n // RAW + 1))
                    act.wait_ge(s_used, i * JOB_SLOTS + n - SPLIT + 1)
                    a(w_hi[:, n % SPLIT, :], raw[:, n % RAW, :], ACT.Copy).then_inc(s_hi, 1)
                    nxt[0] += 1

            def job_high(c):
                act.wait_ge(s_tp, i * 7 + 11 + c + 1)
                a(at_hi[:, 4 * c * P:(4 * c + 4) * P], B[4 + c % 2][:, :], ACT.Copy).then_inc(s_tph, 1)

            act.wait_ge(s_gs, i + 1)
            act.wait_ge(s_mul, i * 7 + 12)
            a(gcol[:], B[6][:, 2 * P:2 * P + 1], ACT.Copy).then_inc(s_gc, 1)
            split(TURN)
            act.wait_ge(s_xu, i * 4 + 12)
            a(selt[:], B[6][:, 0:2 * P], ACT.Copy).then_inc(s_sgc, 1)
            for c in range(7):
                split(4 * c + 1 + AHEAD)
                act.wait_ge(s_used, i * JOB_SLOTS + N0 + 4 * c + 2)
                act.wait_ge(s_mul, i * 7 + 12 + c)
                a(sg[:, 0, :], B[0][:, :], ACT.Silu).then_inc(s_silu, 1)
                if c:
                    job_high(c - 1)
                split(4 * c + 3 + AHEAD)
            split(28 + AHEAD)
            job_high(6)
            split(28 + 2 + AHEAD)
            gathered_rows(i * 2 + 2)
            split(28 + 4 + AHEAD)
            gathered_high(i * 2 + 2)
            split(JOB_SLOTS - 1 + AHEAD)
            for h in range(2):
                if h == 0:
                    act.wait_ge(s_y, i + 10)
                else:
                    act.wait_ge(s_used, (i + 1) * JOB_SLOTS + N0)
                a(y_hi[:, h * 512:(h + 1) * 512], B[2 + h][:, :], ACT.Copy).then_inc(s_yh, 1)
            split(JOB_SLOTS - 1 + TURN)
        act.wait_ge(s_scat, jobs * 4)
        squares(4, jobs * 4 + 8)

    @block.vector
    def _(dve):
        v = nc.vector
        done, ch = [0], [0]

        def split_to(m):
            while done[0] <= min(m, N0 - 1 + TURN):
                n = done[0]
                dve.wait_ge(s_hi, n + 1)
                v.tensor_tensor(w_lo[:, n % SPLIT, :], raw[:, n % RAW, :], w_hi[:, n % SPLIT, :].bitcast(F32),
                                ALU.subtract).then_inc(s_lo, 1)
                done[0] += 1

        def split_half(n, second):
            dve.wait_ge(s_hi if second else s_hh, n + 1 if second else 1)
            w = slice(1024 * second, 1024 * second + 1024)
            ins = v.tensor_tensor(w_lo[:, n % SPLIT, w], raw[:, n % RAW, w], w_hi[:, n % SPLIT, w].bitcast(F32), ALU.subtract)
            if second:
                ins.then_inc(s_lo, 1)
                done[0] += 1

        def step(ins):
            ch[0] += 1
            ins.then_inc(s_dc, 1)
            dve.wait_ge(s_dc, ch[0])

        def normed(i):
            for t in range(NT):
                dve.wait_ge(s_rstd, NT * i + t + 1)
                v.tensor_scalar(xn[:, t, :], xs[:, t, :], stats[:, 4 * i + 2 + t:4 * i + 3 + t], None,
                                ALU.mult).then_inc(s_xn, 1)

        def ht_low(p, gain, banks=(0, 1, 2, 3)):
            for b in range(4):
                dve.wait_ge(s_hth, 8 * p + 2 * b + 2)
                for k in (2 * b, 2 * b + 1):
                    v.scalar_tensor_tensor(ht_lo[:, k, :], B[banks[b]][:, (k % 2) * 256:(k % 2) * 256 + 256],
                                           pk[:, C_GAIN + 8 * gain + k:C_GAIN + 8 * gain + k + 1],
                                           ht_hi[:, k, :].bitcast(F32), ALU.mult, ALU.subtract).then_inc(s_htl, 1)

        def residual(stage, banks, last_slot):
            for n, b in enumerate(banks):
                t, half = divmod(n, 2)
                if n < 3:
                    dve.wait_ge(s_y, 3 * stage + n + 1)
                else:
                    dve.wait_ge(s_used, last_slot + 1)
                xv = xs[:, t, half * 512:(half + 1) * 512]
                v.tensor_tensor(xv, xv, B[b][:, :], ALU.add).then_inc(s_xu, 1)

        normed(0)
        dve.wait_ge(s_wshi, 1)
        v.tensor_tensor(ws_lo[:].rearrange("p k n -> p (k n)"), pk[:, C_WS:C_END],
                        ws_hi[:].rearrange("p k n -> p (k n)").bitcast(F32), ALU.subtract).then_inc(s_wslo, 1)
        ht_low(0, 0)

        def gate_rows():
            dve.wait_ge(s_gp, 1)
            step(v.tensor_scalar(rows[:, 0, :], B[4][0:4, 0:T], pk[0:4, C_BIF:C_BIF + 1], None, ALU.add))
            step(v.tensor_scalar(rows[:, 1, :], B[4][32:36, 0:T], pk[0:4, C_BIF + 1:C_BIF + 2], None, ALU.add))
            v.scalar_tensor_tensor(rows[:, 2, :], rows[:, 1, :], -1.0, rows[:, 1, :], ALU.mult, ALU.max).then_inc(s_lnx, 1)
            dve.wait_ge(s_lnx, 1)
            step(v.tensor_scalar(rows[:, 1, :], rows[:, 1, :], 0.0, None, ALU.min))

        def gate_scans():
            dve.wait_ge(s_lnd, 1)
            step(v.tensor_tensor(rows[:, 1, :], rows[:, 1, :], rows[:, 2, :], ALU.subtract))
            step(v.tensor_tensor_scan(rows[:, 3, :], ones[0:4, 0:1].broadcast_to([4, T]), rows[:, 1, :], 0.0,
                                      ALU.mult, ALU.add))
            step(v.tensor_tensor(rows[:, 4, :], rows[:, 0, :], rows[:, 3, :], ALU.subtract))
            step(v.tensor_tensor_scan(rows[:, 5, :], rows[:, 4, :], rows[:, 4, :], 0.0, ALU.max, ALU.max))
            v.tensor_tensor(rows[:, 6, :], rows[:, 3, :], rows[:, 5, :], ALU.add).then_inc(s_rows, 1)

        for s in range(8):
            split_to(s + AHEAD)
            dve.wait_ge(s_qka, 2 * s + 2)
            for j in (1, 2, 3):
                for b in (0, 1):
                    blk = 2 * s + b
                    if j > 1:
                        dve.wait_ge(s_dc, ch[0] - 1)
                    ins = v.scalar_tensor_tensor(
                        qk[:, blk, j:T], B[s % 3][:, b * 256:b * 256 + T - j],
                        pk[:, C_CONV + 4 * blk + 3 - j:C_CONV + 4 * blk + 4 - j], qk[:, blk, j:T], ALU.mult, ALU.add)
                    if j < 3 or b == 0:
                        ch[0] += 1
                        ins.then_inc(s_dc, 1)
            ins.then_inc(s_conv, 1)
            if s == 1:
                gate_rows()
            if s == 2:
                gate_scans()
        split_to(V0 + AHEAD - 1)
        for h in range(HA):
            dve.wait_ge(s_nm, 1)
            src = B[6 + h // 2][:, (h % 2) * T:(h % 2) * T + T]
            v.tensor_tensor(wd[:, h, 0:T], src, tri_mask[:, :], ALU.add).then_inc(s_arg, 1)
            v.tensor_tensor(wd[:, h, T:384], src[:, P:T], tri_mask[:, 0:P], ALU.add).then_inc(s_arg, 1)
        split_to(O0 + AHEAD - 1)

        def weighted(h):
            dve.wait_ge(s_s, h + 1)
            dve.wait_ge(s_wd, 2 * h + 2)
            if h >= 2:
                dve.wait_ge(s_num, h - 1)
            v.scalar_tensor_tensor(pd[:, h % 2, :], B[4 + h % 2][:, 0:384], DA ** -0.5, wd[:, h, :],
                                   ALU.mult, ALU.mult).then_inc(s_p, 1)

        def inv_den(h):
            dve.wait_ge(s_num, h + 1)
            for t in range(NT):
                if h:
                    dve.wait_ge(s_hs, 2 * h)
                den, lim = num_banks(h)[t][:, DA:DA + 1], small[:, 24 + 4 * t + h:25 + 4 * t + h]
                size = stats[:, 54 + t:55 + t]
                step(v.scalar_tensor_tensor(size, den, -1.0, lim, ALU.mult, ALU.max))
                step(v.tensor_tensor(size, size, den, ALU.max))
            v.reciprocal(stats[:, 52:54], stats[:, 54:56]).then_inc(s_den, 1)

        weighted(0)
        for h in range(HA):
            if h + 1 < HA:
                weighted(h + 1)
            if h < 3:
                split_to(O0 + h + AHEAD)
            inv_den(h)
        for b in range(2):
            dve.wait_ge(s_hr, b + 1)
            dve.wait_ge(s_oc, 2 * b + 2)
            for t in range(NT):
                for h in (2 * b, 2 * b + 1):
                    xv = xn[:, t, h * DA:(h + 1) * DA]
                    col = 44 + 4 * b + 2 * (h % 2) + t
                    ins = v.scalar_tensor_tensor(xv, xv, stats[:, col:col + 1], og[:, t, h * DA:(h + 1) * DA],
                                                 ALU.mult, ALU.mult)
                    if h == 3:
                        dve.wait_ge(s_dc, ch[0])
                        ins.then_inc(s_xn, 1)
                    else:
                        ins.then_inc(s_dc, 1)
                        ch[0] += 1
        ht_low(1, 1)
        split_to(FF0 - 2 + AHEAD)
        residual(0, (4, 5, 6, 7), FF0 - 1)
        normed(1)
        ht_low(2, 2)

        def dense_low(c):
            for b in range(2 if c < 5 else 1):
                dve.wait_ge(s_tph, 2 * c + b + 1)
                dst = slice((4 * c + 2 * b) * T, (4 * c + 2 * b + 2) * T)
                v.tensor_tensor(at_lo[:, dst], B[4 + b][:, :], at_hi[:, dst].bitcast(F32), ALU.subtract).then_inc(s_tpl, 1)

        for c in range(6):
            n = FF0 + 4 * c
            width = 512 if c < 5 else 256
            split_to(n + (1 if c < 5 else 0) + AHEAD)
            if c:
                dense_low(c - 1)
            split_to(n + (3 if c < 5 else 1) + AHEAD)
            for t in range(NT):
                tile_ready(dve, s_u, c, t, n + (3 if c < 5 else 1))
                dve.wait_ge(s_silu, 2 * c + t + 1)
                if c:
                    dve.wait_ge(s_tp, 2 * c)
                v.tensor_tensor(av[:, t, 0:width], sg[:, t, 0:width], B[2 + t][:, 0:width], ALU.mult).then_inc(s_mul, 1)
        dense_low(5)
        split_to(KV0 - 2 + AHEAD)
        residual(1, (0, 1, 2, 3), KV0 - 1)
        normed(2)
        ht_low(3, 3)
        def token_blocks():
            for c in range(2):
                dve.wait_ge(s_kva, 2 * c + 2)
                dve.wait_ge(s_kvd, 2 * c + 2)
                dst = xf[:, 960 * c:960 * c + 960].rearrange("p (j n) -> p j n", j=16)
                for g in range(G):
                    src = ct[:, c, g, :]
                    blocks = bass.AP(src.tensor, src.offset, [list(src.ap[0]), [2, 16], [CS, NC_]])
                    pos = pk[:, C_POS + 16 * c:C_POS + 16 * c + 16].rearrange("p (j o) -> p j o", o=1).broadcast_to([P, 16, NC_])
                    ins = v.tensor_tensor(dst[:, :, g * NC_:(g + 1) * NC_], blocks, pos, ALU.add)
                    if g == G - 1:
                        dve.wait_ge(s_dc, ch[0])
                        ins.then_inc(s_xf, 1)
                    else:
                        ins.then_inc(s_dc, 1)
                        ch[0] += 1

        for i in range(6):
            split_to(KV0 + i + AHEAD)
            if i < 4:
                dve.wait_ge(s_used, KV0 + i + 1)
                upper = B[4 + i % 2][64:128, :].rearrange("p (b t) -> p b t", b=2)
                if i < 2:
                    v.tensor_copy(ct[0:64, i, 1::2, :], upper).then_inc(s_kvd, 1)
                    v.tensor_copy(ct[64:128, i, 1::2, 0:T - 1], upper[:, :, 1:T]).then_inc(s_kvd, 1)
                else:
                    v.tensor_copy(kt[0:64, i - 2, 1::2, :], upper).then_inc(s_kvd, 1)
                    v.tensor_copy(kt[64:128, i - 2, 1::2, :], upper).then_inc(s_kvd, 1)
            if i == 2:
                token_blocks()
            if i == 4:
                dve.wait_ge(s_xch, 1)
                v.tensor_tensor(xc_lo[:], xf[:], xc_hi[:].bitcast(F32), ALU.subtract).then_inc(s_xf, 1)
        ht_low(4, 4)
        split_to(Q0 + 2 + AHEAD)
        dve.wait_ge(s_ng, 1)
        for n, col in enumerate((8, 36)):
            v.tensor_tensor(gat[:, :, 24 * n:24 * n + 24],
                            B[2][:, T:T + 2 * WS].rearrange("p (t n) -> p t n", t=2)[:, :, col:col + 24],
                            pk[:, C_BG + 24 * n:C_BG + 24 * n + 24].rearrange("p (o n) -> p o n", o=1)
                            .broadcast_to([P, 2, 24]), ALU.add).then_inc(s_ngb, 1)
        dve.wait_ge(s_nge, 1)
        g96 = gat[:].rearrange("p t n -> p (t n)")
        step(v.tensor_scalar(g96, g96, 1.0, None, ALU.add))
        step(v.reciprocal(g96, g96))
        split_to(Q0 + 3 + AHEAD)

        def cmp_bias(t):
            dve.wait_ge(s_cs, 2 * t + 2)
            if t:
                dve.wait_ge(s_ct, t)
            p = pc[:, :, 0:NC_]
            step(v.tensor_tensor(p, B[7][:, :].rearrange("p (h n) -> p h n", n=32)[:, :, 0:NC_], dcb[:, t, :, :], ALU.add))
            step(v.tensor_reduce(cmx[:, 0, :], p, AX.X, ALU.max))
            v.tensor_tensor(p, p, cmx[:, 0, :].rearrange("p (h o) -> p h o", o=1).broadcast_to([P, HB, NC_]),
                            ALU.subtract).then_inc(s_cb, 1)

        def cmp_sums(t):
            dve.wait_ge(s_ce, t + 1)
            p = pc[:, :, 0:NC_]
            step(v.tensor_tensor(p, p, cval[:, t, :].rearrange("p (o n) -> p o n", o=1).broadcast_to([P, HB, NC_]),
                                 ALU.mult))
            step(v.tensor_reduce(cmx[:, 1, :], p, AX.X, ALU.add))

        def cmp_probs(t):
            p = pc[:, :, 0:NC_]
            step(v.tensor_scalar(cmx[:, 1, :], cmx[:, 1, :], 1e-30, None, ALU.max))
            step(v.reciprocal(cmx[:, 1, :], cmx[:, 1, :]))
            gv = gat[:, t, :].rearrange("p (h b) -> p h b", b=3)
            step(v.tensor_tensor(cmx[:, 1, :], cmx[:, 1, :], gv[:, :, 0], ALU.mult))
            v.tensor_tensor(p, p, cmx[:, 1, :].rearrange("p (h o) -> p h o", o=1).broadcast_to([P, HB, NC_]),
                            ALU.mult).then_inc(s_cp, 1)

        def head_bias(n):
            t, h = divmod(n, HB)
            lk = P * (t + 1)
            dve.wait_ge(s_as, n + 1)
            if n >= SC:
                dve.wait_ge(s_at, n - SC + 1)
            dst = sc[:, n % SC, 0:2 * lk].rearrange("p (b k) -> p b k", b=2)
            step(v.scalar_tensor_tensor(
                dst, dat[:, t, 0:lk].rearrange("p (o k) -> p o k", o=1).broadcast_to([P, 2, lk]),
                float(2.0 ** (-8.0 * (h + 1) / HB)), B[n % 3][:, 0:2 * lk].rearrange("p (b k) -> p b k", b=2),
                ALU.mult, ALU.add))
            v.tensor_reduce(att[:, 0, :, n:n + 1], dst, AX.X, ALU.max, negate=True).then_inc(s_ab, 1)

        def head_scale(n):
            t, h = divmod(n, HB)
            lk = P * (t + 1)
            dve.wait_ge(s_ae, 2 * n + 2)
            step(v.reciprocal(coef[:, :, n:n + 1], att[:, 1, :, n:n + 1]))
            v.tensor_tensor(coef[:, :, n:n + 1], coef[:, :, n:n + 1],
                            gat[:, t, 3 * h + 1:3 * h + 3].rearrange("p (b o) -> p b o", o=1), ALU.mult).then_inc(s_cf, 1)
            dve.wait_ge(s_cf, n + 1)
            last = sc[:, n % SC, lk:2 * lk]
            v.tensor_scalar(last, last, coef[:, 1, n:n + 1], None, ALU.mult).then_inc(s_scd, 1)

        def group_low(grp):
            t, g = divmod(grp, G)
            dve.wait_ge(s_aoh, 2 * grp + 2)
            for odd in range(2):
                dst = (slice(64 * odd, 64 * odd + 64), slice(2 * g, 2 * g + 2), slice(t * P, (t + 1) * P))
                v.tensor_tensor(ht_lo[dst], B[4 + grp % 2][0:64, :].rearrange("p (k o q) -> p o k q", k=2, o=2)[:, odd, :, :],
                                ht_hi[dst].bitcast(F32), ALU.subtract).then_inc(s_aol, 1)

        dve.wait_ge(s_const, 4)
        head_bias(0)
        head_bias(1)
        for n in range(2 * HB):
            t, h = divmod(n, HB)
            head_scale(n)
            if n + 2 < 2 * HB:
                head_bias(n + 2)
            if n in (1, 13):
                cmp_bias(n // 13)
            if n in (2, 15):
                cmp_sums(n // 15)
            if n in (2, 16):
                cmp_probs(n // 16)
            if n > 2 * R and n % R == 2:
                group_low(n // R - 2)
            if n in (25, 27):
                split_half(BO0 + 2, n == 27)
        group_low(2 * G - 2)
        split_to(BO0 + 3)
        group_low(2 * G - 1)
        split_to(N0 - 2 + AHEAD)
        residual(2, (0, 1, 2, 7), N0 - 1)
        normed(3)
        split_to(N0 - 1 + AHEAD)
        ht_low(5, 6)
        dve.wait_ge(s_xt, 24)
        dve.wait_ge(s_g1b, 16)
        for t in range(NT):
            v.tensor_tensor(xn[:, t, :], xn[:, t, :], g1b[:], ALU.mult).then_inc(s_hgx, 1)
        def one_hot(j):
            for t in range(NT):
                v.tensor_tensor(sel_oh[:, t, :], slot_iota[:], posj[:, t, j].broadcast_to([P, P]),
                                ALU.is_equal).then_inc(s_sel, 1)

        r = [rt[:, k, :].rearrange("p (t e) -> p t e", t=NT) for k in range(16)]
        rf = [rt[:, k, :] for k in range(16)]
        L = r[0]
        dve.wait_ge(s_lg, 1)
        step(v.tensor_copy(L, B[4][:, T:T + NT * WS].rearrange("p (t e) -> p t e", t=NT)[:, :, 64:64 + NE]))
        wins = big8[:, 0, :].rearrange("p (t e f) -> p t e f", t=NT, e=NE)
        ties = big8[:, 1, :].rearrange("p (t e f) -> p t e f", t=NT, e=NE)
        for t in range(NT):
            mine = L[:, t, :].rearrange("p (e o) -> p e o", o=1).broadcast_to([P, NE, NE])
            other = L[:, t, :].rearrange("p (o e) -> p o e", o=1).broadcast_to([P, NE, NE])
            v.tensor_tensor(wins[:, t, :, :], other, mine, ALU.is_gt).then_inc(s_dc, 1)
            v.tensor_tensor(ties[:, t, :, :], other, mine, ALU.is_equal).then_inc(s_dc, 1)
            ch[0] += 2
        step(v.tensor_reduce(r[4][:, :, 0], L, AX.X, ALU.max))
        v.tensor_tensor(r[1], L, r[4][:, :, 0:1].broadcast_to([P, NT, NE]), ALU.subtract).then_inc(s_le, 1)
        step(v.tensor_tensor(ties, ties, tri8[:].rearrange("p (o e) f -> p o e f", o=1).broadcast_to([P, NT, NE, NE]), ALU.mult))
        step(v.tensor_tensor(wins, wins, ties, ALU.add))
        step(v.tensor_reduce(r[3], wins, AX.X, ALU.add))
        v.tensor_scalar(rf[5], rf[3], 2.0, None, ALU.is_lt).then_inc(s_selm, 1)
        for t in range(NT):
            dve.wait_ge(s_hgh, t + 1)
            v.tensor_tensor(hg_lo[:, t, :], xn[:, t, :], hg_hi[:, t, :].bitcast(F32), ALU.subtract).then_inc(s_hgl, 1)
        dve.wait_ge(s_rank, 1)
        cnt = r[7][:, 0, :]
        step(v.tensor_copy(rt[:, 6:8, :].rearrange("p a b -> p (a b)")[:, 0:NT * NE + NE], B[1][:, 0:NT * NE + NE]))
        dve.wait_ge(s_selm, 1)
        step(v.scalar_tensor_tensor(rf[6], rf[6], 1.0, rf[5], ALU.add, ALU.mult))
        step(v.tensor_scalar(posj[:, :, 0:NE], r[6], -1.0, None, ALU.add))
        one_hot(slice(0, 1))
        dve.wait_ge(s_lex, 1)
        step(v.tensor_tensor(rf[2], rf[2], rf[5], ALU.mult))
        step(v.tensor_reduce(r[4][:, :, 1], r[2], AX.X, ALU.add))
        step(v.reciprocal(r[4][:, :, 2], r[4][:, :, 1]))
        v.tensor_tensor(gatej[:, :, 0:NE], r[2], r[4][:, :, 2:3].broadcast_to([P, NT, NE]), ALU.mult).then_inc(s_gates, 1)
        dve.wait_ge(s_gates, 1)
        over, rank = r[8][:, 0, :], r[8][:, 1, :]
        v.memset(posj[:, :, NJ_MAX:12], -1.0).then_inc(s_dc, 1)
        v.memset(gatej[:, :, NJ_MAX:12], 0.0).then_inc(s_dc, 1)
        v.memset(rf[15], 0.0).then_inc(s_dc, 1)
        ch[0] += 3
        step(v.tensor_scalar(over, cnt, float(P), None, ALU.is_gt))
        step(v.tensor_tensor_scan(rank, ones[:, 0:NE], over, 0.0, ALU.mult, ALU.add))
        nk = NJ_MAX - NE
        pick = big8[:, 0, 0:nk * NE].rearrange("p (k e) -> p k e", k=nk)
        work = big8[:, 1, 0:NT * nk * NE].rearrange("p (t k e) -> p t k e", t=NT, k=nk)
        num = iot[:, 1:1 + nk].rearrange("p (k o) -> p k o", o=1).broadcast_to([P, nk, NE])

        def over_k(v_):
            return v_.rearrange("p (o e) -> p o e", o=1).broadcast_to([P, nk, NE])

        step(v.tensor_tensor(pick, over_k(rank), num, ALU.is_equal))
        step(v.tensor_tensor(pick, pick, over_k(over), ALU.mult))
        step(v.tensor_tensor(work[:, 0, :, :], pick, over_k(iot[:]), ALU.mult))
        v.tensor_scalar(rf[15][0:1, 0:1], rank[0:1, NE - 1:NE], float(NE), None, ALU.add).then_inc(s_dc, 1)
        ch[0] += 1
        step(v.tensor_reduce(rf[15][0:1, 1:1 + nk], work[0:1, 0, :, :], AX.X, ALU.add))
        pick_t = pick.rearrange("p (o k) e -> p o k e", o=1).broadcast_to([P, NT, nk, NE])
        for table, less in ((posj, -float(P)), (gatej, 0.0)):
            step(v.tensor_tensor(work, pick_t, table[:, :, 0:NE].rearrange("p t (o e) -> p t o e", o=1)
                                 .broadcast_to([P, NT, nk, NE]), ALU.mult))
            dst = table[:, :, NE:NJ_MAX]
            step(v.tensor_reduce(dst, work, AX.X, ALU.add))
            if less:
                step(v.tensor_scalar(dst, dst, less, None, ALU.add))
        v.tensor_copy(tab[0:1, 0:16], rf[15][0:1, 0:16]).then_inc(s_tab, 1)

        def gathered_low(n):
            for h in range(2):
                dve.wait_ge(s_gah, n + h + 1)
                v.tensor_tensor(ht_lo[:, 2 * h:2 * h + 2, :].rearrange("p k t -> p (k t)"), B[4 + h][:, :],
                                ht_hi[:, 2 * h:2 * h + 2, :].rearrange("p k t -> p (k t)").bitcast(F32),
                                ALU.subtract).then_inc(s_gal, 1)

        gathered_low(0)
        split_to(N0 - 1 + TURN)
        dve.wait_ge(s_tab, 1)
        jobs = dve.value_load(tab[0:1, 0:1], min_val=NE, max_val=NJ_MAX)
        with dve.Fori(0, jobs) as i:
            nxt = [TURN]

            def split(m):
                while nxt[0] <= m:
                    n = N0 + nxt[0]
                    dve.wait_ge(s_hi, i * JOB_SLOTS + n + 1)
                    v.tensor_tensor(w_lo[:, n % SPLIT, :], raw[:, n % RAW, :], w_hi[:, n % SPLIT, :].bitcast(F32),
                                    ALU.subtract).then_inc(s_lo, 1)
                    nxt[0] += 1

            def job_low(c):
                dve.wait_ge(s_tph, i * 7 + 11 + c + 1)
                dst = slice(4 * c * P, (4 * c + 4) * P)
                v.tensor_tensor(at_lo[:, dst], B[4 + c % 2][:, :], at_hi[:, dst].bitcast(F32), ALU.subtract).then_inc(s_tpl, 1)

            for c in range(7):
                split(4 * c + 1 + AHEAD)
                if c:
                    job_low(c - 1)
                split(4 * c + 3 + AHEAD)
                if c == 0:
                    dve.wait_ge(s_gc, i + 1)
                dve.wait_ge(s_used, i * JOB_SLOTS + N0 + 4 * c + 4)
                dve.wait_ge(s_silu, i * 7 + 12 + c + 1)
                dve.wait_ge(s_tp, i * 7 + 11 + c)
                v.scalar_tensor_tensor(av[:, 0, :], sg[:, 0, :], gcol[:, 0:1], B[1][:, :],
                                       ALU.mult, ALU.mult).then_inc(s_mul, 1)
            dve.wait_ge(s_gs, i + 1)
            one_hot(bass.ds(i + 1, 1))
            split(28 + AHEAD)
            job_low(6)
            split(28 + 4 + AHEAD)
            gathered_low(i * 2 + 2)
            split(JOB_SLOTS - 2 + AHEAD)
            for h in range(2):
                dve.wait_ge(s_yh, i * 2 + h + 1)
                v.tensor_tensor(y_lo[:, h * 512:(h + 1) * 512], B[2 + h][:, :], y_hi[:, h * 512:(h + 1) * 512].bitcast(F32),
                                ALU.subtract).then_inc(s_yl, 1)
            split(JOB_SLOTS - 1 + AHEAD)
            for n, b in enumerate((1, 7, 5, 2)):
                t, half = divmod(n, 2)
                dve.wait_ge(s_scat, i * 4 + n + 1)
                dve.wait_ge(s_xu, i * 4 + 9 + n)
                xv = xs[:, t, half * 512:(half + 1) * 512]
                v.tensor_tensor(xv, xv, B[b][:, :], ALU.add).then_inc(s_xu, 1)
            split(JOB_SLOTS - 1 + TURN)
        dve.wait_ge(s_gfb, 16)
        for t in range(NT):
            dve.wait_ge(s_rstd, 4 * NT + t + 1)
            v.scalar_tensor_tensor(xn[:, t, :], xs[:, t, :], stats[:, 18 + t:19 + t], gfb[:], ALU.mult,
                                   ALU.mult).then_inc(s_fin, 1)

    @block.tensor
    def _(pe):
        mm = nc.tensor.matmul

        def mm3(out_, sh, sl, mh, ml, first, last):
            mm(out_, sh, mh, start=first, stop=False)
            mm(out_, sh, ml, start=False, stop=False)
            return mm(out_, sl, mh, start=False, stop=last)

        def wait_slot(n, i=None):
            pe.wait_ge(s_lo, (n if i is None else i * JOB_SLOTS + n) + 1)

        def transposed(p, xn_count, banks=(0, 1, 2, 3)):
            for t in range(NT):
                pe.wait_ge(s_xn, xn_count - NT + t + 1)
                for k in range(KD):
                    ins = nc.tensor.transpose(B[banks[k // 2]][:, (k % 2) * 256 + t * P:(k % 2) * 256 + (t + 1) * P],
                                              xn[:, t, k * P:(k + 1) * P], ident[:])
                    if t == NT - 1 and k % 2:
                        ins.then_inc(s_xt, 1)

        def fresh_k(fresh, k, n=1):
            if fresh is not None:
                pe.wait_ge(s_htl, 8 * fresh + k + n)

        def hth(k, t):
            return ht_hi[:, k, t * P:(t + 1) * P]

        def htl(k, t):
            return ht_lo[:, k, t * P:(t + 1) * P]

        def features(n, bank, fresh=None):
            wait_slot(n)
            for b in range(2):
                for k in range(KD):
                    if b == 0:
                        fresh_k(fresh, k)
                    ins = mm3(bank[:, b * 256:b * 256 + 256], weights(w_hi, n, 256)[:, k, b * P:(b + 1) * P],
                              weights(w_lo, n, 256)[:, k, b * P:(b + 1) * P], ht_hi[:, k, :], ht_lo[:, k, :],
                              k == 0, k == KD - 1)
            ins.then_inc(s_used, 1)

        def wide(n, b, banks, kt0, nkt, first, last, sem_, hi=hth, lo=htl, fresh=None):
            wait_slot(n)
            for t in range(NT):
                for k in range(nkt):
                    if t == 0:
                        fresh_k(fresh, kt0 + k)
                    ins = mm3(B[banks[t]][:, 0:b], hi(kt0 + k, t), lo(kt0 + k, t), weights(w_hi, n, b)[:, k, :],
                              weights(w_lo, n, b)[:, k, :], first and k == 0, last and k == nkt - 1)
                if last and t == 0:
                    ins.then_inc(sem_, 1)
            ins.then_inc(s_used, 1)

        def down(n, banks, kt0, first, last, hi=hth, lo=htl, fresh=None):
            wait_slot(n)
            fresh_k(fresh, kt0, 2)
            for t in range(NT):
                for half in range(2):
                    for k in range(2):
                        w = slice(half * 512, half * 512 + 512)
                        ins = mm3(B[banks[2 * t + half]][:, :], hi(kt0 + k, t), lo(kt0 + k, t),
                                  weights(w_hi, n, 1024)[:, k, w], weights(w_lo, n, 1024)[:, k, w],
                                  first and k == 0, last and k == 1)
                    if last and 2 * t + half < 3:
                        ins.then_inc(s_y, 1)
            ins.then_inc(s_used, 1)

        def small_features(bank, fresh=None):
            for k in range(KD):
                fresh_k(fresh, k)
                ins = mm3(bank[0:WS, 0:T], ws_hi[:, k, :], ws_lo[:, k, :], ht_hi[:, k, :], ht_lo[:, k, :],
                          k == 0, k == KD - 1)
            return ins

        def small_tokens(bank, src):
            for t in range(NT):
                ins = nc.tensor.transpose(bank[:, T + t * WS:T + (t + 1) * WS], src[:, t * P:(t + 1) * P],
                                          ident[0:WS, 0:WS])
            return ins

        pe.wait_ge(s_const, 1)
        transposed(0, 2)
        pe.wait_ge(s_wslo, 1)
        small_features(B[4], 0).then_inc(s_gp, 1)
        for s in range(8):
            if s >= 3:
                pe.wait_ge(s_conv, s - 2)
            features(QK0 + s, B[s % 3])
            if s == 4:
                pe.wait_ge(s_rows, 2)
                for row, c0 in ((4, 0), (7, 8)):
                    for t in range(NT):
                        ins = nc.tensor.transpose(B[5][:, c0 + 4 * t:c0 + 4 * t + 4],
                                                  rows[:, row, t * P:(t + 1) * P], ident[0:4, 0:4])
                ins.then_inc(s_cols, 1)
                for h in range(HA):
                    ins = mm(B[6 + h // 2][:, (h % 2) * T:(h % 2) * T + T], nsel[:, h, :], rows[:, 5, :],
                             start=True, stop=True)
                ins.then_inc(s_nm, 1)
        for c in range(2):
            pe.wait_ge(s_conv, 6 + 2 * c)
            for half in range(2):
                wide(V0 + 2 * c + half, 512, (2 - 2 * c, 3 - 2 * c), 4 * half, 4, half == 0, half == 1, s_v)

        def scores(h):
            if h == 0:
                pe.wait_ge(s_conv, 8)
                pe.wait_ge(s_colc, 1)
            if h >= 2:
                pe.wait_ge(s_p, h - 1)
            bank = B[4 + h % 2]
            for d in range(2):
                mm(bank[:, 0:T], qk[:, 8 + 2 * h + d, 0:P], qk[:, 2 * h + d, :], start=d == 0, stop=d == 1)
            for d in range(2):
                ins = mm(bank[:, T:384], qk[:, 8 + 2 * h + d, P:T], qk[:, 2 * h + d, P:T], start=d == 0, stop=d == 1)
            ins.then_inc(s_s, 1)

        def numerator(h):
            pe.wait_ge(s_p, h + 1)
            pe.wait_ge(s_vc, 4)
            if h == 0:
                pe.wait_ge(s_arg, 8)
            elif h < 3:
                pe.wait_ge(s_hs, 2 * h)
            p = pd[:, h % 2, :]
            n0, n1 = num_banks(h)
            mm(n0[:, 0:DA + 1], p[:, 0:P], va[:, 0, h, :], start=True, stop=True)
            mm(n1[:, 0:DA + 1], p[:, P:T], va[:, 0, h, :], start=True, stop=False)
            mm(n1[:, 0:DA + 1], p[:, T:384], va[:, 1, h, :], start=False, stop=True).then_inc(s_num, 1)

        scores(0)
        scores(1)
        pe.wait_ge(s_vc, 2)
        for h in range(HA):
            if h == 2:
                pe.wait_ge(s_vc, 4)
            c, half = divmod(h, 2)
            if h < 3:
                wide(O0 + h, 512, (2 - 2 * c, 3 - 2 * c), 4 * half, 4, half == 0, half == 1, s_o)
            numerator(h)
            if h + 2 < HA:
                scores(h + 2)
        wide(O0 + 3, 512, (0, 1), 4, 4, False, True, s_o)
        pe.wait_ge(s_oc, 4)
        transposed(1, 4)
        for k in range(4):
            down(WO0 + k, (4, 5, 6, 7), 2 * k, k == 0, k == 3, fresh=1)
        transposed(2, 6)
        def dense_t(c):
            pe.wait_ge(s_mul, 2 * c + 2)
            for b in range(2 if c < 5 else 1):
                if c:
                    pe.wait_ge(s_tpl, 2 * (c - 1) + b + 1)
                for j in range(2):
                    for t in range(NT):
                        blk = 2 * b + j
                        ins = nc.tensor.transpose(B[4 + b][:, j * 256 + t * P:j * 256 + (t + 1) * P],
                                                  av[:, t, blk * P:(blk + 1) * P], ident[:])
                ins.then_inc(s_tp, 1)

        for c in range(6):
            n = FF0 + 4 * c
            if c:
                pe.wait_ge(s_silu, 2 * c)
            else:
                pe.wait_ge(s_htl, 18)
            if c < 5:
                for half in range(2):
                    wide(n + half, 512, (0, 1), 4 * half, 4, half == 0, half == 1, s_g, fresh=None if c else 2)
            else:
                wide(n, 256, (0, 1), 0, 8, True, True, s_g)
            if c:
                dense_t(c - 1)
                pe.wait_ge(s_mul, 2 * c)
            if c < 5:
                for half in range(2):
                    wide(n + 2 + half, 512, (2, 3), 4 * half, 4, half == 0, half == 1, s_u)
            else:
                wide(n + 1, 256, (2, 3), 0, 8, True, True, s_u)
        dense_t(5)

        def ath(k, t):
            return at_hi[:, k * T + t * P:k * T + (t + 1) * P]

        def atl(k, t):
            return at_lo[:, k * T + t * P:k * T + (t + 1) * P]

        pe.wait_ge(s_silu, 12)
        for k in range(11):
            pe.wait_ge(s_tpl, min(k + 1, 11))
            down(DN0 + k, (0, 1, 2, 3), 2 * k, k == 0, k == 10, ath, atl)
        transposed(3, 8)
        for i in range(6):
            if i >= 2:
                pe.wait_ge(s_kva, 2 * (i - 1))
                pe.wait_ge(s_kvd, 2 * (i - 1))
            bank = B[4 + i % 2]
            n = KV0 + i
            if i < 4:
                features(n, bank, None if i else 3)
            else:
                wait_slot(n)
                for t in range(NT):
                    for k in range(KD):
                        ins = mm3(bank[:, t * 256:(t + 1) * 256], hth(k, t), htl(k, t), weights(w_hi, n, 256)[:, k, :],
                                  weights(w_lo, n, 256)[:, k, :], k == 0, k == KD - 1)
                ins.then_inc(s_used, 1)
        transposed(4, 8)
        for c in range(2):
            if c == 0:
                pe.wait_ge(s_xf, 3)
            for half in range(2):
                n = W10 + 2 * c + half
                wait_slot(n)
                for j in range(8):
                    jj = 8 * half + j
                    at = 960 * c + 60 * jj
                    ins = mm3(B[6 + c][0:XM, 0:CH], xc_hi[:, at:at + XM], xc_lo[:, at:at + XM],
                              weights(w_hi, n, CH)[:, j, :], weights(w_lo, n, CH)[:, j, :], jj == 0, jj == 15)
                ins.then_inc(s_used, 1)
        pe.wait_ge(s_hid, 2)
        pe.wait_ge(s_kva, 12)
        for c in range(2):
            for hb in range(2):
                ins = nc.tensor.transpose(B[4][:, (2 * c + hb) * 60:(2 * c + hb) * 60 + 60],
                                          hid[:, c, hb * P:(hb + 1) * P], ident[0:G * NC_, 0:G * NC_])
        ins.then_inc(s_hidt, 1)
        features(Q0, B[0], 4)
        pe.wait_ge(s_hidc, 1)
        w2 = pk[:, C_W2:C_W2 + 256].rearrange("p (c h d) -> p c h d", c=2, h=2)
        for top in (0, 64):
            for hb in range(2):
                mm(B[5][top:top + 64, 0:G * NC_], w2[:, 0, hb, :], hidt[:, 0, hb, :], start=hb == 0, stop=hb == 1)
        for g in range(G):
            for hb in range(2):
                ins = mm(B[6][0:NC_, g * DB:(g + 1) * DB], hidt[:, 1, hb, g * NC_:(g + 1) * NC_], w2[:, 1, hb, :],
                         start=hb == 0, stop=hb == 1)
        ins.then_inc(s_w2, 1)
        for i in range(1, 4):
            if i >= 2:
                pe.wait_ge(s_qc, i - 1)
            features(Q0 + i, B[i % 2])
            if i == 1:
                small_features(B[2]).then_inc(s_sf, 1)
            if i == 2:
                pe.wait_ge(s_sfc, 1)
                small_tokens(B[2], sc[0:WS, 2, 0:T]).then_inc(s_ng, 1)
        pe.wait_ge(s_kc, 5)

        def cmp_scores(t, odd, pairs):
            for pair in pairs:
                h = 2 * pair + odd
                lo = 64 * odd
                g = h // R
                ins = mm(B[7][:, h * 32:h * 32 + NC_], qt[lo:lo + 64, pair, t * P:(t + 1) * P],
                         kc[lo:lo + 64, g * NC_:(g + 1) * NC_], start=True, stop=True)
            if pairs[-1] == HB // 2 - 1:
                ins.then_inc(s_cs, 1)
                if odd == 0:
                    pe.wait_ge(s_cs, 2 * t + 1)

        def cmp_transpose(t):
            pe.wait_ge(s_cp, t + 1)
            for g in range(G):
                ins = nc.tensor.transpose(B[7][:, g * P:(g + 1) * P],
                                          pc[:, g * R:(g + 1) * R, :].rearrange("p h n -> p (h n)"), ident[:])
            ins.then_inc(s_ct, 1)

        def head_scores(n):
            t, h = divmod(n, HB)
            lk = P * (t + 1)
            lo = 64 * (h % 2)
            if n >= 3:
                pe.wait_ge(s_ab, n - 2)
            mm(B[n % 3][:, 0:2 * lk], qt[lo:lo + 64, h // 2, t * P:(t + 1) * P], kt[lo:lo + 64, :, h // R, 0:lk],
               start=True, stop=True).then_inc(s_as, 1)

        def head_transpose(n):
            blocks = 2 * (n // HB + 1)
            pe.wait_ge(s_sca, n + 1)
            pe.wait_ge(s_scd, n + 1)
            if n >= 2:
                pe.wait_ge(s_atc, n - 1)
            for b in range(blocks):
                ins = nc.tensor.transpose(B[(3, 6)[n % 2]][:, b * P:(b + 1) * P], sc[:, n % SC, b * P:(b + 1) * P], ident[:])
            ins.then_inc(s_at, 1)

        def group_part(grp, j):
            t, g = divmod(grp, G)
            if j == 0:
                pe.wait_ge(s_atc, R * (grp + 1))
                if g == 0:
                    pe.wait_ge(s_ctc, t + 1)
                if grp >= 2:
                    pe.wait_ge(s_aol, 2 * (grp - 1))
            bank = B[4 + grp % 2]
            if j < 2 * (t + 1):
                b, k = divmod(j, t + 1)
                mm(bank[0:64, :], vv[:, k, b, g * DB:(g + 1) * DB], ptg[grp % 2][:, j, :, :]
                   .rearrange("p r q -> p (r q)"), start=j == 0, stop=False)
            ins = mm(bank[0:64, j * P:(j + 1) * P], vbd[:, g, j * DB:(j + 1) * DB], pct[:, t, g * P:(g + 1) * P],
                     start=False, stop=j == R - 1)
            if j == R - 1:
                ins.then_inc(s_av, 1)

        pe.wait_ge(s_qc, 4)
        pe.wait_ge(s_ngb, 2)
        for n in range(3):
            head_scores(n)
        cmp_scores(0, 0, range(HB // 2))
        cmp_scores(0, 1, range(HB // 2))
        for n in range(2 * HB):
            if n + 3 < 2 * HB:
                head_scores(n + 3)
            if n > R:
                group_part((n - 1) // R - 1, (n - 1) % R)
            if n == 5:
                pe.wait_ge(s_ctc, 1)
            if 5 <= n < 13:
                cmp_scores(1, (n - 5) // 4, range(2 * ((n - 5) % 4), 2 * ((n - 5) % 4) + 2))
            head_transpose(n)
            if n in (3, 17):
                cmp_transpose(n // 17)
        group_part(2 * G - 2, R - 1)
        for k in range(4):
            pe.wait_ge(s_aol, 10 + 2 * k)
            down(BO0 + k, (0, 1, 2, 7), 2 * k, k == 0, k == 3)
            if k == 0:
                for j in range(R):
                    group_part(2 * G - 1, j)
        transposed(5, 10)
        small_features(B[4], 5).then_inc(s_sf, 1)
        pe.wait_ge(s_sfc, 2)
        small_tokens(B[4], small[0:WS, 0:T]).then_inc(s_lg, 1)
        pe.wait_ge(s_selm, 1)
        c0, c1 = rt[:, 5, 0:NE], rt[:, 5, NE:2 * NE]
        mm(B[1][:, 0:NE], tri1[:], c0, start=True, stop=True)
        mm(B[1][:, NE:2 * NE], ones[:], c0, start=True, stop=False)
        mm(B[1][:, NE:2 * NE], tri1[:], c1, start=False, stop=True)
        mm(B[1][:, 2 * NE:3 * NE], ones[:], c0, start=True, stop=False)
        mm(B[1][:, 2 * NE:3 * NE], ones[:], c1, start=False, stop=True).then_inc(s_rank, 1)

        def gather(sel_count):
            pe.wait_ge(s_sel, sel_count)
            for h in range(2):
                for t in range(NT):
                    for part in (hg_hi, hg_lo):
                        ins = mm(B[h][:, :], sel_oh[:, t, :], part[:, t, h * 512:(h + 1) * 512],
                                 start=t == 0 and part is hg_hi, stop=t == 1 and part is hg_lo)
                ins.then_inc(s_ga, 1)

        def places(job):
            for t in range(NT):
                mm(B[6][:, 2 * P:2 * P + 1], sel_oh[:, t, :].bitcast(F32), gatej[:, t, job], start=t == 0, stop=t == 1)
            for t in range(NT):
                ins = nc.tensor.transpose(B[6][:, t * P:(t + 1) * P], sel_oh[:, t, :].bitcast(F32), ident[:])
            ins.then_inc(s_gs, 1)

        def gather_t(n):
            for h in range(2):
                pe.wait_ge(s_gr, n + h + 1)
                for k in range(4):
                    ins = nc.tensor.transpose(B[4 + h][:, k * P:(k + 1) * P],
                                              rows_g[:, (4 * h + k) * P:(4 * h + k + 1) * P], ident[:])
                ins.then_inc(s_gt, 1)

        def gu(s, bank, i=None):
            n = N0 + s
            wait_slot(n, i)
            half = s % 2
            for k in range(4):
                kk = 4 * half + k
                hi = ht_hi[:, kk // 2, (kk % 2) * P:(kk % 2) * P + P]
                lo = ht_lo[:, kk // 2, (kk % 2) * P:(kk % 2) * P + P]
                ins = mm3(bank[:, :], hi, lo, weights(w_hi, n, 512)[:, k, :], weights(w_lo, n, 512)[:, k, :],
                          kk == 0, kk == 7)
            ins.then_inc(s_used, 1)

        pe.wait_ge(s_hgl, 2)
        gather(2)
        gather_t(0)
        pe.wait_ge(s_gates, 1)
        places(slice(0, 1))
        pe.wait_ge(s_gal, 1)
        gu(0, B[0])
        pe.wait_ge(s_gal, 2)
        pe.wait_ge(s_tab, 1)
        jobs = pe.value_load(tab[0:1, 0:1], min_val=NE, max_val=NJ_MAX)
        with pe.Fori(0, jobs) as i:
            def job_t(c):
                pe.wait_ge(s_mul, i * 7 + 12 + c + 1)
                if c >= 2:
                    pe.wait_ge(s_tpl, i * 7 + 11 + c - 1)
                for j in range(4):
                    ins = nc.tensor.transpose(B[4 + c % 2][:, j * P:(j + 1) * P], av[:, 0, j * P:(j + 1) * P], ident[:])
                ins.then_inc(s_tp, 1)

            for c in range(7):
                if c:
                    pe.wait_ge(s_silu, i * 7 + 12 + c)
                    gu(4 * c, B[0], i)
                gu(4 * c + 1, B[0], i)
                if c:
                    job_t(c - 1)
                    pe.wait_ge(s_mul, i * 7 + 12 + c)
                else:
                    pe.wait_ge(s_xu, i * 4 + 9)
                gu(4 * c + 2, B[1], i)
                gu(4 * c + 3, B[1], i)
                if c == 0:
                    pe.wait_ge(s_xu, i * 4 + 12)
            for d in range(14):
                if d == 1:
                    job_t(6)
                if d == 3:
                    gather(i * 2 + 4)
                    pe.wait_ge(s_sgc, i + 1)
                    places(bass.ds(i + 1, 1))
                if d == 5:
                    pe.wait_ge(s_tpl, i * 7 + 11 + 7)
                    gather_t(i * 2 + 2)
                n = N0 + 28 + d
                wait_slot(n, i)
                if d < 12:
                    pe.wait_ge(s_tpl, i * 7 + 11 + d // 2 + 1)
                for half in range(2):
                    for k in range(2):
                        kk = 2 * d + k
                        w = slice(half * 512, half * 512 + 512)
                        ins = mm3(B[2 + half][:, :], at_hi[:, kk * P:(kk + 1) * P], at_lo[:, kk * P:(kk + 1) * P],
                                  weights(w_hi, n, 1024)[:, k, w], weights(w_lo, n, 1024)[:, k, w],
                                  d == 0 and k == 0, d == 13 and k == 1)
                    if d == 13 and half == 0:
                        ins.then_inc(s_y, 1)
                ins.then_inc(s_used, 1)
            pe.wait_ge(s_gal, i * 2 + 4)
            gu(0, B[0], i + 1)
            for n, b in enumerate((1, 7, 5, 2)):
                t, half = divmod(n, 2)
                pe.wait_ge(s_yl, i * 2 + half + 1)
                sel = selt[:, t * P:(t + 1) * P]
                mm(B[b][:, :], sel, y_hi[:, half * 512:(half + 1) * 512], start=True, stop=False)
                mm(B[b][:, :], sel, y_lo[:, half * 512:(half + 1) * 512], start=False, stop=True).then_inc(s_scat, 1)

    ctx.close()


def kernel(**inputs):
    import numpy as np
    from concourse import bacc
    from concourse.bass_utils import run_bass_kernel_spmd

    f = {k: np.asarray(v) for k, v in inputs.items()}

    def columns(v):
        return v.reshape(KD, P).T

    gains = [f["norm_mix"][0], f["a_norm_h"][0], f["norm_ffn"][0], f["norm_kv"], f["norm_mix"][1],
             np.ones(D, np.float32), f["norm_ffn"][1]]
    packed = np.zeros((P, C_END), np.float32)
    for n, g in enumerate(gains):
        packed[:, C_GAIN + 8 * n:C_GAIN + 8 * n + 8] = columns(g)
    packed[:, C_CONV:C_CONV + 64] = f["a_conv"][0].reshape(4, 16, P).transpose(2, 1, 0).reshape(P, 64)
    packed[0:4, C_BIF] = f["a_b_gate"][0, 0:4]
    packed[0:4, C_BIF + 1] = f["a_b_gate"][0, 4:8]
    packed[:, C_BG:C_BG + 48] = f["b_b_gate"][0][None, :]
    packed[:, C_POS:C_POS + 32] = f["b_cmp_pos"].reshape(16, 2, 2, DB).transpose(1, 3, 2, 0).reshape(P, 32)
    packed[:, C_W2:C_W2 + 256] = f["b_cmp_w2"].reshape(2, 2, P, DB).transpose(2, 0, 1, 3).reshape(P, 256)
    ws = np.zeros((D, WS), np.float32)
    ws[:, 0:4], ws[:, 32:36] = f["a_w_in"][0][:, 4 * D:4 * D + 4], f["a_w_in"][0][:, 4 * D + 4:]
    ws[:, 8:32], ws[:, 36:60] = f["b_w_q"][0][:, D:D + 24], f["b_w_q"][0][:, D + 24:]
    ws[:, 64:72] = f["m_router"][0]
    packed[:, C_WS:C_END] = ws.reshape(KD, P, WS).transpose(1, 0, 2).reshape(P, KD * WS)

    arrays = {"x": f["x"], "packed": packed, "a_w_in": f["a_w_in"], "a_w_out": f["a_w_out"], "b_w_kv": f["b_w_kv"],
              "b_cmp_w1": f["b_cmp_w1"], "b_w_q": f["b_w_q"], "b_w_out": f["b_w_out"], "f_w_gu": f["f_w_gu"],
              "f_w_down": f["f_w_down"], "m_w_gu": f["m_w_gu"], "m_w_down": f["m_w_down"],
              "norm_ffn1": f["norm_ffn"][1:2], "norm_final": f["norm_final"][None, :]}
    arrays = {k: np.ascontiguousarray(v) for k, v in arrays.items()}
    nc = bacc.Bacc("TRN2", target_bir_lowering=False, num_devices=1)
    aps = [nc.dram_tensor(f"in_{k}", v.shape, mybir.dt.float32, kind="ExternalInput").ap() for k, v in arrays.items()]
    out = nc.dram_tensor("out", (1, T, D), mybir.dt.float32, kind="ExternalOutput").ap()
    trunk(nc, *aps, out)
    r = run_bass_kernel_spmd(nc, [{f"in_{k}": v for k, v in arrays.items()}], core_ids=[0])
    return r.results[0]["out"]
```
